# Optimizing a Trainium2 kernel written in Bass

```python
import math
import jax
import jax.numpy as jnp
from jax import lax
import numpy as np

D_MODEL = 2048
BATCH = 1
SEQ = 256
DEPTH = 1
DEC_BATCH = 8
DEC_SEQ = 1
PAST_LEN = 1024
PAGE_SIZE = 128

EPS = 1e-6
NEG_INF = -1e30
F32 = jnp.float32

POOL_WINDOWS = (2, 4, 8, 16)
POOL_GROUP = D_MODEL // 8
POOL_WIDTH = POOL_GROUP * len(POOL_WINDOWS)
POOL_HIST = max(POOL_WINDOWS) - 1

DIL_CONFIGS = ((128, 1), (512, 4), (2048, 16))
N_DIL = len(DIL_CONFIGS)
DIL_HEAD_DIM = 128
DIL_HEADS = D_MODEL // 256
DIL_WIDTH = DIL_HEADS * DIL_HEAD_DIM
DIL_BLOCK = 128

GLA_HEADS = 4
GLA_KEY_WIDTH = D_MODEL // 2
GLA_VAL_WIDTH = D_MODEL
GLA_DK = GLA_KEY_WIDTH // GLA_HEADS
GLA_DV = GLA_VAL_WIDTH // GLA_HEADS
GLA_RANK = 16
GLA_TAU = 16.0
GLA_CHUNK = 64

N_BRANCH = 3
COL_SIZES = (POOL_WIDTH,) + (DIL_WIDTH,) * (3 * N_DIL) + (GLA_KEY_WIDTH, GLA_KEY_WIDTH, GLA_VAL_WIDTH, GLA_VAL_WIDTH, GLA_RANK, N_BRANCH * D_MODEL)
N_IN = sum(COL_SIZES)

REL_BUCKETS = 32
REL_MAX_DIST = 2048
N_REL_HEADS = N_DIL * DIL_HEADS

MEM_LEN = 256
X_HEADS = 4
X_HEAD_DIM = D_MODEL // 8
X_WIDTH = X_HEADS * X_HEAD_DIM

D_FF = 11 * D_MODEL // 4
FFN_CONV = 3

kernel_name = 'hybrid_pool_dilated_gla_decoder_step'

def rmsnorm(x, g):
    x32 = x.astype(F32)
    y = x32 * lax.rsqrt(jnp.mean(x32 * x32, axis=-1, keepdims=True) + EPS) * g.astype(F32)
    return y.astype(x.dtype)

def rel_bucket(dist):
    max_exact = REL_BUCKETS // 2
    scaled = jnp.log(jnp.maximum(dist, 1).astype(F32) / max_exact) / math.log(REL_MAX_DIST / max_exact)
    large = jnp.minimum(max_exact + (scaled * (REL_BUCKETS - max_exact)).astype(jnp.int32), REL_BUCKETS - 1)
    return jnp.where(dist < max_exact, dist, large)

def dilated_slot_biases(rel_bias):
    out = []
    for g, (win, dil) in enumerate(DIL_CONFIGS):
        dist = jnp.arange(win // dil + 1, dtype=jnp.int32) * dil
        b = rel_bias[rel_bucket(dist), g * DIL_HEADS:(g + 1) * DIL_HEADS]
        out.append(b.T.astype(F32))
    return out

def pool_mix(u_ctx, pos0, pool_w, pool_scale):
    B_, Lc, _ = u_ctx.shape
    T = Lc - POOL_HIST
    cs = jnp.pad(jnp.cumsum(u_ctx.astype(F32), axis=1), ((0, 0), (1, 0), (0, 0)))
    pos = pos0 + jnp.arange(T)
    u = u_ctx[:, POOL_HIST:].astype(F32)
    end = POOL_HIST + 1
    outs = []
    for g, w in enumerate(POOL_WINDOWS):
        sl = slice(g * POOL_GROUP, (g + 1) * POOL_GROUP)
        win_sum = cs[:, end:end + T, sl] - cs[:, end - w:end - w + T, sl]
        cnt = jnp.minimum(w, pos + 1).astype(F32)[None, :, None]
        outs.append(win_sum / cnt - u[..., sl])
    d = jnp.stack(outs, axis=2)
    y = jnp.einsum('btgc,gcd->btgd', d, pool_w.astype(F32)).reshape(B_, T, POOL_WIDTH) * pool_scale.astype(F32)
    return y.astype(u_ctx.dtype)

def dilated_attn_prompt(q, k, v, dil, n_slots, bias_hj):
    B_, S_, H, E = q.shape
    L = S_ // dil
    nb = -(-L // DIL_BLOCK)
    Lp = nb * DIL_BLOCK

    def to_sub(t):
        t = t.reshape(B_, L, dil, H, E).transpose(0, 2, 1, 3, 4)
        return jnp.pad(t, ((0, 0), (0, 0), (0, Lp - L), (0, 0), (0, 0)))

    def band(t):
        t = jnp.pad(t, ((0, 0), (0, 0), (DIL_BLOCK, 0), (0, 0), (0, 0))).reshape(B_, dil, nb + 1, DIL_BLOCK, H, E)
        return jnp.concatenate([t[:, :, :-1], t[:, :, 1:]], axis=3)

    qb = to_sub(q).reshape(B_, dil, nb, DIL_BLOCK, H, E)
    kb = band(to_sub(k))
    vb = band(to_sub(v))
    s = jnp.einsum('bdnqhe,bdnkhe->bdnhqk', qb, kb, preferred_element_type=F32) * DIL_HEAD_DIM ** -0.5
    qi = jnp.arange(DIL_BLOCK)[:, None] + DIL_BLOCK
    ki = jnp.arange(2 * DIL_BLOCK)[None, :]
    rel = qi - ki
    key_ok = (jnp.arange(nb)[:, None, None] * DIL_BLOCK + ki[None] - DIL_BLOCK) >= 0
    ok = (rel >= 0) & (rel <= n_slots) & key_ok
    s = s + bias_hj[:, jnp.clip(rel, 0, n_slots)][None, None, None]
    s = jnp.where(ok[None, None, :, None], s, NEG_INF)
    lse = jax.nn.logsumexp(s, axis=-1)
    p = jnp.exp(s - lse[..., None])
    o = jnp.einsum('bdnhqk,bdnkhe->bdnqhe', p, vb.astype(F32))
    o = o.reshape(B_, dil, Lp, H, E)[:, :, :L].transpose(0, 2, 1, 3, 4).reshape(B_, S_, H, E)
    lse = lse.transpose(0, 1, 2, 4, 3).reshape(B_, dil, Lp, H)[:, :, :L].transpose(0, 2, 1, 3).reshape(B_, S_, H)
    return o, lse

def dilated_attn_step(q, kc, vc, dil, n_slots, bias_hj, n_past):
    T = q.shape[1]
    idx = n_past + jnp.arange(T)[:, None] - jnp.arange(n_slots + 1)[None, :] * dil
    ok = idx >= 0
    idx = jnp.maximum(idx, 0)
    kg = kc[:, idx]
    vg = vc[:, idx]
    s = jnp.einsum('bthe,btjhe->bthj', q, kg, preferred_element_type=F32) * DIL_HEAD_DIM ** -0.5 + bias_hj[None, None]
    s = jnp.where(ok[None, :, None, :], s, NEG_INF)
    lse = jax.nn.logsumexp(s, axis=-1)
    p = jnp.exp(s - lse[..., None])
    o = jnp.einsum('bthj,btjhe->bthe', p, vg.astype(F32))
    return o, lse

def gla_chunked(q, k, v, log_a):
    B_, T, H, K = q.shape
    V = v.shape[-1]
    C = GLA_CHUNK
    n = T // C
    q, k, v, log_a = [t.reshape(B_, n, C, H, t.shape[-1]) for t in (q, k, v, log_a)]
    b = jnp.cumsum(log_a, axis=2)
    b_last = b[:, :, -1:]
    q_t = q * jnp.exp(b)
    k_t = k * jnp.exp(-b)
    k_h = k * jnp.exp(b_last - b)
    decay = jnp.exp(b_last[:, :, 0])
    A = jnp.einsum('bnchk,bnshk->bnhcs', q_t, k_t)
    A = jnp.where(jnp.tril(jnp.ones((C, C), dtype=bool)), A, 0.0)
    o_intra = jnp.einsum('bnhcs,bnshv->bnchv', A, v)

    def step(S, xs):
        qc, kc, vc, dc = xs
        o = jnp.einsum('bchk,bhkv->bchv', qc, S)
        S = dc[..., None] * S + jnp.einsum('bchk,bchv->bhkv', kc, vc)
        return S, o

    S0 = jnp.zeros((B_, H, K, V), F32)
    S, o_inter = lax.scan(step, S0, (jnp.moveaxis(q_t, 1, 0), jnp.moveaxis(k_h, 1, 0), jnp.moveaxis(v, 1, 0), jnp.moveaxis(decay, 1, 0)))
    o = o_intra + jnp.moveaxis(o_inter, 0, 1)
    return o.reshape(B_, T, H, V), S

def gla_step(q, k, v, log_a, S):
    def step(S, xs):
        qt, kt, vt, at = xs
        S = jnp.exp(at)[..., None] * S + kt[..., None] * vt[..., None, :]
        return S, jnp.einsum('bhk,bhkv->bhv', qt, S)

    S, o = lax.scan(step, S.astype(F32), tuple(jnp.moveaxis(t, 1, 0) for t in (q, k, v, log_a)))
    return jnp.moveaxis(o, 0, 1), S

def token_mixer(h, w_in, pool_w, pool_scale, gla_w_a2, gla_b_a, gla_norm, w_br_pool, w_br_dil, w_br_gla, w_mix_out, biases, hist, pos0):
    B_, T, _ = h.shape
    z = jnp.einsum('btd,dn->btn', h, w_in)
    points = [int(c) for c in np.cumsum(COL_SIZES)[:-1]]
    parts = jnp.split(z, points, axis=-1)
    u_pool = parts[0]
    dil_parts = parts[1:1 + 3 * N_DIL]
    gq, gk, gv, gr, ga, gates = parts[1 + 3 * N_DIL:]
    prompt = hist is None
    if prompt:
        pool_hist = jnp.zeros((B_, POOL_HIST, POOL_WIDTH), u_pool.dtype)
    else:
        pool_hist, dil_hists, gla_state = hist

    u_ctx = jnp.concatenate([pool_hist.astype(u_pool.dtype), u_pool], axis=1)
    y_pool = pool_mix(u_ctx, pos0, pool_w, pool_scale)
    new_pool = u_ctx[:, -POOL_HIST:]

    outs, lses, new_dil = [], [], []
    for g, (win, dil) in enumerate(DIL_CONFIGS):
        q, k, v = [t.reshape(B_, T, DIL_HEADS, DIL_HEAD_DIM) for t in dil_parts[3 * g:3 * g + 3]]
        if prompt:
            o, lse = dilated_attn_prompt(q, k, v, dil, win // dil, biases[g])
            new_dil.append(jnp.stack([k, v], axis=2)[:, -min(win, T):])
        else:
            kv_hist = dil_hists[g]
            kc = jnp.concatenate([kv_hist[:, :, 0], k.astype(kv_hist.dtype)], axis=1)
            vc = jnp.concatenate([kv_hist[:, :, 1], v.astype(kv_hist.dtype)], axis=1)
            o, lse = dilated_attn_step(q.astype(kv_hist.dtype), kc, vc, dil, win // dil, biases[g], kv_hist.shape[1])
            new_dil.append(jnp.stack([k, v], axis=2).astype(kv_hist.dtype))
        outs.append(o)
        lses.append(lse)
    wts = jax.nn.softmax(jnp.stack(lses, axis=0), axis=0)
    y_dil = jnp.sum(wts[..., None] * jnp.stack(outs, axis=0), axis=0).reshape(B_, T, DIL_WIDTH).astype(h.dtype)

    q = (gq.astype(F32) * GLA_DK ** -0.5).reshape(B_, T, GLA_HEADS, GLA_DK)
    k = gk.astype(F32).reshape(B_, T, GLA_HEADS, GLA_DK)
    v = gv.astype(F32).reshape(B_, T, GLA_HEADS, GLA_DV)
    log_a = jax.nn.log_sigmoid(jnp.einsum('btr,rk->btk', ga.astype(F32), gla_w_a2.astype(F32)) + gla_b_a.astype(F32)) / GLA_TAU
    log_a = log_a.reshape(B_, T, GLA_HEADS, GLA_DK)
    if prompt:
        o, S = gla_chunked(q, k, v, log_a)
        new_gla = S.astype(h.dtype)
    else:
        o, S = gla_step(q, k, v, log_a, gla_state)
        new_gla = S.astype(gla_state.dtype)
    o = o * lax.rsqrt(jnp.mean(o * o, axis=-1, keepdims=True) + EPS) * gla_norm.astype(F32).reshape(GLA_HEADS, GLA_DV)
    y_gla = (o.reshape(B_, T, GLA_VAL_WIDTH) * jax.nn.silu(gr.astype(F32))).astype(h.dtype)

    bp = jnp.einsum('btc,cd->btd', y_pool, w_br_pool).astype(F32)
    bd = jnp.einsum('btc,cd->btd', y_dil, w_br_dil).astype(F32)
    bg = jnp.einsum('btc,cd->btd', y_gla, w_br_gla).astype(F32)
    gate = jax.nn.sigmoid(gates.astype(F32)).reshape(B_, T, N_BRANCH, D_MODEL)
    merged = gate[:, :, 0] * bp + gate[:, :, 1] * bd + gate[:, :, 2] * bg
    y = jnp.einsum('btd,de->bte', merged.astype(h.dtype), w_mix_out)
    return y, new_pool, new_dil, new_gla

def memory_kv(mem, g, w_xkv):
    B_, M, _ = mem.shape
    kv = jnp.einsum('bmd,dn->bmn', rmsnorm(mem, g), w_xkv)
    return kv.reshape(B_, M, 2, X_HEADS, X_HEAD_DIM)

def cross_attn(h, mem_kv, w_xq, w_xo):
    B_, T, _ = h.shape
    q = jnp.einsum('btd,dn->btn', h, w_xq).reshape(B_, T, X_HEADS, X_HEAD_DIM)
    s = jnp.einsum('bthe,bmhe->bhtm', q, mem_kv[:, :, 0].astype(q.dtype), preferred_element_type=F32) * X_HEAD_DIM ** -0.5
    p = jax.nn.softmax(s, axis=-1)
    o = jnp.einsum('bhtm,bmhe->bthe', p, mem_kv[:, :, 1].astype(F32))
    return jnp.einsum('btn,nd->btd', o.reshape(B_, T, X_WIDTH).astype(h.dtype), w_xo)

def conv_ffn(h, w_up, conv_w, conv_b, w_down, conv_hist):
    B_, T, _ = h.shape
    u = jnp.einsum('btd,df->btf', h, w_up)
    if conv_hist is None:
        conv_hist = jnp.zeros((B_, FFN_CONV - 1, 2 * D_FF), u.dtype)
    u_ctx = jnp.concatenate([conv_hist.astype(u.dtype), u], axis=1)
    c = conv_b.astype(F32)
    for i in range(FFN_CONV):
        c = c + conv_w[i].astype(F32) * u_ctx[:, i:i + T].astype(F32)
    gate, val = jnp.split(c, 2, axis=-1)
    y = jnp.einsum('btf,fd->btd', (jax.nn.gelu(gate) * val).astype(h.dtype), w_down)
    return y, u_ctx[:, -(FFN_CONV - 1):]

def decoder_layer(x, mem_kv, hist, conv_hist, pos0, biases, lw):
    (n_mix_pre, n_mix_post, w_in, pool_w, pool_scale, gla_w_a2, gla_b_a, gla_norm, w_br_pool, w_br_dil, w_br_gla, w_mix_out,
     n_x_pre, n_x_post, w_xq, w_xo, n_ffn_pre, n_ffn_post, w_up, conv_w, conv_b, w_down) = lw
    y, new_pool, new_dil, new_gla = token_mixer(rmsnorm(x, n_mix_pre), w_in, pool_w, pool_scale, gla_w_a2, gla_b_a, gla_norm,
                                                w_br_pool, w_br_dil, w_br_gla, w_mix_out, biases, hist, pos0)
    x = x + rmsnorm(y, n_mix_post)
    x = x + rmsnorm(cross_attn(rmsnorm(x, n_x_pre), mem_kv, w_xq, w_xo), n_x_post)
    y, new_conv = conv_ffn(rmsnorm(x, n_ffn_pre), w_up, conv_w, conv_b, w_down, conv_hist)
    x = x + rmsnorm(y, n_ffn_post)
    return x, new_pool, new_dil, new_gla, new_conv

def setup_inputs(seed: int = 0) -> dict:
    key = jax.random.key(seed)
    keys = jax.random.split(key, 48)
    counter = iter(range(48))

    def nrm(shape, scale=1.0):
        return jax.random.normal(keys[next(counter)], shape, jnp.float32) * scale

    def gain(shape):
        return 1.0 + nrm(shape, 0.05)

    L = DEPTH
    x_prompt = nrm((BATCH, SEQ, D_MODEL))
    x_sample = nrm((DEC_BATCH, DEC_SEQ, D_MODEL))
    state_pool = nrm((L, DEC_BATCH, POOL_HIST, POOL_WIDTH))
    dil_caches = [nrm((L, DEC_BATCH, min(win, PAST_LEN), 2, DIL_HEADS, DIL_HEAD_DIM)) for (win, _) in DIL_CONFIGS]
    state_gla = nrm((L, DEC_BATCH, GLA_HEADS, GLA_DK, GLA_DV))
    cache_mem_kv = nrm((L, DEC_BATCH, MEM_LEN, 2, X_HEADS, X_HEAD_DIM))
    state_ffn_conv = nrm((L, DEC_BATCH, FFN_CONV - 1, 2 * D_FF))
    mem_prompt = nrm((BATCH, MEM_LEN, D_MODEL))
    return {
        'x_prompt': x_prompt,
        'x_sample': x_sample,
        'state_pool': state_pool,
        'cache_dil1_kv': dil_caches[0],
        'cache_dil2_kv': dil_caches[1],
        'cache_dil3_kv': dil_caches[2],
        'state_gla': state_gla,
        'cache_mem_kv': cache_mem_kv,
        'state_ffn_conv': state_ffn_conv,
        'mem_prompt': mem_prompt,
        'rel_bias': nrm((REL_BUCKETS, N_REL_HEADS), 0.2),
        'norm_mix_pre': gain((L, D_MODEL)),
        'norm_mix_post': gain((L, D_MODEL)),
        'w_in': nrm((L, D_MODEL, N_IN), D_MODEL ** -0.5),
        'pool_w': nrm((L, len(POOL_WINDOWS), POOL_GROUP, POOL_GROUP), POOL_GROUP ** -0.5),
        'pool_scale': 1.0 + nrm((L, POOL_WIDTH), 0.1),
        'gla_w_a2': nrm((L, GLA_RANK, GLA_KEY_WIDTH), GLA_RANK ** -0.5),
        'gla_b_a': nrm((L, GLA_KEY_WIDTH), 0.01),
        'gla_norm': gain((L, GLA_VAL_WIDTH)),
        'w_br_pool': nrm((L, POOL_WIDTH, D_MODEL), POOL_WIDTH ** -0.5),
        'w_br_dil': nrm((L, DIL_WIDTH, D_MODEL), DIL_WIDTH ** -0.5),
        'w_br_gla': nrm((L, GLA_VAL_WIDTH, D_MODEL), GLA_VAL_WIDTH ** -0.5),
        'w_mix_out': nrm((L, D_MODEL, D_MODEL), D_MODEL ** -0.5),
        'norm_x_pre': gain((L, D_MODEL)),
        'norm_x_post': gain((L, D_MODEL)),
        'norm_mem': gain((L, D_MODEL)),
        'w_xq': nrm((L, D_MODEL, X_WIDTH), D_MODEL ** -0.5),
        'w_xkv': nrm((L, D_MODEL, 2 * X_WIDTH), D_MODEL ** -0.5),
        'w_xo': nrm((L, X_WIDTH, D_MODEL), X_WIDTH ** -0.5),
        'norm_ffn_pre': gain((L, D_MODEL)),
        'norm_ffn_post': gain((L, D_MODEL)),
        'w_up': nrm((L, D_MODEL, 2 * D_FF), D_MODEL ** -0.5),
        'conv_w': nrm((L, FFN_CONV, 2 * D_FF), FFN_CONV ** -0.5),
        'conv_b': nrm((L, 2 * D_FF), 0.01),
        'w_down': nrm((L, D_FF, D_MODEL), D_FF ** -0.5),
    }

def reference(x_prompt, x_sample, state_pool, cache_dil1_kv, cache_dil2_kv, cache_dil3_kv, state_gla, cache_mem_kv, state_ffn_conv,
              mem_prompt, rel_bias, norm_mix_pre, norm_mix_post, w_in, pool_w, pool_scale, gla_w_a2, gla_b_a, gla_norm,
              w_br_pool, w_br_dil, w_br_gla, w_mix_out, norm_x_pre, norm_x_post, norm_mem, w_xq, w_xkv, w_xo,
              norm_ffn_pre, norm_ffn_post, w_up, conv_w, conv_b, w_down):
    biases = dilated_slot_biases(rel_bias)
    dil_caches = (cache_dil1_kv, cache_dil2_kv, cache_dil3_kv)
    xp, xs = x_prompt, x_sample
    pool_p, gla_p, mem_p, conv_p = [], [], [], []
    pool_s, gla_s, conv_s = [], [], []
    dil_p = [[] for _ in range(N_DIL)]
    dil_s = [[] for _ in range(N_DIL)]
    for l in range(DEPTH):
        lw = (norm_mix_pre[l], norm_mix_post[l], w_in[l], pool_w[l], pool_scale[l], gla_w_a2[l], gla_b_a[l], gla_norm[l],
              w_br_pool[l], w_br_dil[l], w_br_gla[l], w_mix_out[l], norm_x_pre[l], norm_x_post[l], w_xq[l], w_xo[l],
              norm_ffn_pre[l], norm_ffn_post[l], w_up[l], conv_w[l], conv_b[l], w_down[l])
        mem_kv_p = memory_kv(mem_prompt, norm_mem[l], w_xkv[l])
        xp, pool_new, dil_new, gla_new, conv_new = decoder_layer(xp, mem_kv_p, None, None, 0, biases, lw)
        pool_p.append(pool_new)
        gla_p.append(gla_new)
        mem_p.append(mem_kv_p)
        conv_p.append(conv_new)
        for g in range(N_DIL):
            dil_p[g].append(dil_new[g])
        hist = (state_pool[l], [c[l] for c in dil_caches], state_gla[l])
        xs, pool_new, dil_new, gla_new, conv_new = decoder_layer(xs, cache_mem_kv[l], hist, state_ffn_conv[l], PAST_LEN, biases, lw)
        pool_s.append(pool_new)
        gla_s.append(gla_new)
        conv_s.append(conv_new)
        for g in range(N_DIL):
            dil_s[g].append(dil_new[g])
    return (xp, xs,
            jnp.stack(pool_p), jnp.stack(dil_p[0]), jnp.stack(dil_p[1]), jnp.stack(dil_p[2]), jnp.stack(gla_p), jnp.stack(mem_p), jnp.stack(conv_p),
            jnp.stack(pool_s), jnp.stack(dil_s[0]), jnp.stack(dil_s[1]), jnp.stack(dil_s[2]), jnp.stack(gla_s), jnp.stack(conv_s))


_drawn_inputs = setup_inputs


def setup_inputs(seed=0):
    import zlib

    import numpy as np

    out = dict(_drawn_inputs(seed))
    spreads = {}
    factors = {'gla_b_a': 8.0, 'conv_b': 7.965}
    for name, (base, spread) in spreads.items():
        noise = np.random.default_rng([zlib.crc32(name.encode()), seed]).standard_normal(out[name].shape)
        drawn = base * np.exp(spread * noise) if base else spread * noise
        out[name] = jnp.asarray(drawn.astype(out[name].dtype))
    for name, factor in factors.items():
        out[name] = (out[name] * factor).astype(out[name].dtype)
    return out
```

```python
from contextlib import ExitStack

import numpy as np
import concourse.bass as bass
from concourse import mybir
from concourse.alu_op_type import AluOpType as ALU

F32 = mybir.dt.float32
F32R = mybir.dt.float32r
ACT = mybir.ActivationFunctionType
AX = mybir.AxisListType
ds = bass.ds

P = 128
D = 2048
NP = 256
NS = 8
T = NP + NS
KB = D // P
SLOT = KB * P
RING = 3
EPS = 1e-6
COL_POOL = 0
COL_DIL = 1024
DIL_W = 1024
COL_GQ = COL_DIL + 9 * DIL_W
COL_GK = COL_GQ + 1024
COL_GV = COL_GK + 1024
COL_GR = COL_GV + 2048
COL_GA = COL_GR + 2048
COL_GATE = COL_GA + 16
DILS = (1, 4, 16)
DSLOTS = (128, 128, 64)
CACHE = (128, 512, 1024)
SSEEN = sum(DSLOTS)
H = 8
E = 128
NEG = -1e30
DF = 5632
FT = DF // P
FH = FT // 2

PC_MIXPRE, PC_MIXPOST, PC_XPRE, PC_XPOST, PC_MEM, PC_FPRE, PC_FPOST = range(0, 112, 16)
PC_PSCALE, PC_BA, PC_GNORM, PC_CW, PC_CB = 112, 120, 128, 144, 408
PC_END = 496


class Steps:

    def __init__(self, sem, names):
        self.sem, self.names = sem, names.split()
        self.n = len(self.names)
        assert len(set(self.names)) == self.n, names
        self.next = 0

    def __call__(self, name):
        assert self.names[self.next] == name, (self.names[self.next], name)
        self.next = (self.next + 1) % self.n
        return self.sem

    def at(self, name, body=0):
        return self.sem, body * self.n + (self.n + self.names.index(name) + 1)


class Phase:

    def __init__(self, book, slots, outs, bodies):
        self.c0, self.slots, self.outs = book["c"], slots, outs
        self.base = dict(book["bank"])
        book["c"] += slots * bodies
        for b in outs:
            book["bank"][b] += bodies
        self.evac = book["evac"]

    def c(self, j, i=0):
        return i * self.slots + (self.c0 + j)

    def s(self, j):
        return (self.c0 + j) % RING

    def third(self, j, i=0):
        return i * (self.slots // RING) + (self.c0 + j) // RING

    def freed(self, k, i=0):
        b = self.outs[k]
        return self.evac[b], i * self.outs.count(b) + (self.base[b] + self.outs[:k].count(b) + 1)

    def saved(self, k, i=0):
        b = self.outs[k]
        return self.evac[b], i * self.outs.count(b) + (self.base[b] + self.outs[:k].count(b) + 2)

    def before(self, b, i=0):
        return self.evac[b], i * self.outs.count(b) + (self.base[b] + 1)


def build(nc, A):
    with ExitStack() as ctx:
        def sem(name):
            return ctx.enter_context(nc.semaphore(name))

        start = -(-nc.sbuf_base // 64) * 64
        arena = ctx.enter_context(nc.sbuf_tensor("arena", [P, (nc.sbuf_usable_end - start) // 4 - 8], F32))
        where = [start]

        def region(size):
            where[0] += size
            return where[0] - size

        def at(name, shape, off, dt=F32):
            return nc.alloc_sbuf_tensor_at(name, shape, dtype=dt, offset=off, align_bytes=8)

        TB = T * 4
        W_RAW, W_HI, W_LO = (region(RING * SLOT * 4) for _ in range(3))
        R_HH, R_HL = (region(KB * TB) for _ in range(2))
        R_YH, R_YL = (region(FH * TB) for _ in range(2))
        R_M = region(KB * TB)
        R_X = region(KB * TB)
        R_CONST = region(512 * 2 + 2048)
        R_Z = region(21984)
        assert where[0] <= nc.sbuf_usable_end, where

        raw = at("weights_raw", [P, RING, SLOT], W_RAW)
        w_hi = at("weights_hi", [P, RING, SLOT], W_HI, F32R)
        w_lo = at("weights_lo", [P, RING, SLOT], W_LO, F32R)
        h_hi = at("h_hi", [P, KB, T], R_HH, F32R)
        h_lo = at("h_lo", [P, KB, T], R_HL, F32R)
        y_hi = at("y_hi", [P, FH, T], R_YH, F32R)
        y_lo = at("y_lo", [P, FH, T], R_YL, F32R)
        merged = at("merged", [P, KB, T], R_M)
        xres = at("x_residual", [P, KB, T], R_X)
        ident = at("identity", [P, P], R_CONST)
        ones = at("ones", [P, P], R_CONST + 512)
        par = at("parameters", [P, 512], R_CONST + 1024)

        prow = at("parameter_rows", [P, 5, P], R_Z)
        onehot = at("onehot", [33, 3 * 383 + SSEEN + 3], R_Z + 2560)
        relx = at("rel_bias_rows", [33, 24], R_Z + 8448)
        toep = at("bias_diagonals", [8, 3, 384], R_Z + 8544)
        sbias_all = at("sample_bias_all", [8, 324], R_Z + 13152)
        scan_keep = at("scan_keep", [P, NP], R_Z + 19584)
        w_a2 = at("w_a2", [16, 1024], R_Z + 15472)
        ga = at("gate_low_rank", [16, T], R_Z + 20608)
        stat = at("row_stats", [P, 16], R_Z + 21728)
        xtok = at("x_tokens", [P, 2, D], R_M)
        xtok_s = at("x_tokens_sample", [NS, D], R_X + 8448)
        junk = [at("squares_unread_a", [P, D], R_HL), at("squares_unread_b", [P, D], R_YH)]

        la = at("gla_log_decay", [P, 8, T], R_X)
        gtmp = at("gla_tmp", [P, 8, T], R_M)
        g_qt = at("gla_q", [P, 2, NP], R_Z)
        g_kt = at("gla_k", [P, 2, NP], R_Z + 2048)
        g_kh = at("gla_k_to_end", [P, 2, NP], R_Z + 4096)
        g_vtok = at("gla_v_tokens", [P, 2, 512], R_Z + 6144)
        g_S = at("gla_state", [P, 2, 512], R_Z + 10240)
        g_at = at("gla_scores", [P, 2, P], R_Z + 14336)
        g_o = at("gla_o", [P, 4, T], R_Z + 15360)
        g_var = at("gla_var", [P, T], R_Z + 19584)
        g_rstd = at("gla_rstd", [P, T], R_Z + 20640)
        g_ks = at("gla_k_sample", [P, 8, NS], R_Z + 21696)
        g_dec = at("gla_chunk_decay", [P, 2, 4], R_Z + 21952)
        g_qs = at("gla_q_sample", [P, 8, NS], R_X + 16640)
        yt1, yt2 = R_YH + KB * TB, R_YL + KB * TB
        g_vT = at("gla_v", [P, 4, T], yt1)
        g_sq = at("gla_o_squared", [P, 4, T], R_Z + 6144)
        g_khtok = at("gla_k_tokens", [P, 2, NP], yt1 + 4224)
        g_sr = at("gla_silu_r", [P, 4, T], yt2)
        g_vs = at("gla_v_sample_tokens", [NS, 512], yt2 + 4224)
        g_Ss = [at(f"gla_state_sample{r}", [P, 2, 512], (R_X + 8448 if r < 2 else R_M) + 4096 * (r % 2))
                for r in range(4)]
        g_vb = at("gla_v_spread", [P, 4, 512], R_M + 8192)
        g_qm = at("gla_q_apart", [P, 2, NS, NS], R_M + 16384)
        g_om = at("gla_o_sample_tokens", [NS, 512], yt2 + 4224)
        gates = at("gates", [P, 4, T], R_Z)


        vcache = at("v_cache", [P, 3, NS, E], R_X)
        s1 = at("scores_late", [P, 3, NP], R_X + 12288)
        s0 = at("scores_early", [P, 3, P], R_X + 15360)
        yt3, yt4 = R_YH + 8 * TB, R_YL + 8 * TB
        kcache = at("k_cache", [P, NS, E], yt3)
        qspread = at("q_spread", [P, NS, E], yt3 + 4096)
        kvtok = at("kv_tokens", [P, 3, 2, 2, E], yt3 + 8192)
        pT = at("probs_turned", [P, 3, 384], yt4)
        qkvs = at("qkv_sample", [NS, 3, 384], yt4 + 4608)
        btab = at("bias_table", [P, 3, NP], yt4 + 9216)
        bsamp = at("bias_sample", [NS, 324], yt4 + 12288)
        qkvT = at("qkv", [P, 9, T], R_Z)
        gates2 = at("gates_dil", [P, 4, T], R_Z + 9504)
        ssamp = at("scores_sample", [NS, 324], R_Z + 13728)
        vnew = at("v_new", [NS, 3, E], R_Z + 15040)
        qk_junk = at("qk_product", [NS, E], R_Z + 16576)
        sct = at("scores_sample_slots", [P, 3, NS], R_Z + 17088)
        psT = at("probs_sample", [P, 3, NS], R_Z + 17184)
        pdiag = at("new_key_probs", [NS, 3, NS], R_Z + 17280)
        snew = at("new_key_scores", [NS, 4], R_Z + 17376)
        dst = at("softmax_stats", [P, 8], R_Z + 17392)
        dss = at("softmax_stats_sample", [NS, 4], R_Z + 17424)
        dtmp = at("gated_dil", [P, 2, T], R_Z + 17440)

        UW, UP, US = 400, 15, 272
        u_ctx = at("pool_context", [P, 4, UW], R_X)
        wsum = [at(f"pool_window_sums{n}", [P, 2, UW], R_X + 6400 + 3200 * n) for n in range(2)]
        pdiff = at("pool_window_mean_less_u", [P, 2, T], R_X + 12800)
        ptok = at("pool_history_rows", [NS * 15, 1024], yt1)
        utok = at("pool_new_rows", [15, 1024], R_Z)
        utok_s = at("pool_new_rows_sample", [NS, 1024], R_Z + 4096)
        cinv = at("pool_counts_inverse", [P, 16], R_Z + 20608)

        hm_hi = at("memory_normed_hi", [P, KB, NP], R_YH, F32R)
        hm_lo = at("memory_normed_lo", [P, KB, NP], R_YL, F32R)
        memtok = at("memory_tokens", [P, 2, D], R_X)
        sqjunk = at("squares_unread", [P, D], R_YL)
        xtok2 = at("x_tokens_again", [P, 2, D], R_Z)
        xtok2_s = [at("x_tokens_sample_a", [NS, 1024], R_YH + 16384), at("x_tokens_sample_b", [NS, 1024], R_YL + 17408)]
        acc = at("squares_sum", [P, T], R_Z + 16384)
        rstd = at("rstd", [P, T], R_Z + 17440)
        sqr = at("squares", [P, 3, T], R_Z + 18496)
        mstat = at("memory_stats", [P, 8], R_Z + 21664)

        kT = [at("mem_k_a", [P, 4, NP], R_YH + 16384), at("mem_k_b", [P, 4, NP], R_YL + 17408)]
        kvtok2 = at("mem_kv_tokens", [P, 2, 2, 1024], R_Z)
        kvr = at("mem_kv_tile", [P, 3, NP], R_Z + 18496)
        qT = at("xq", [P, 4, T], R_Z)
        xp = at("x_probs", [P, 2, NP], R_Z + 4224)
        xpT = at("x_probs_turned", [P, 2, NP], R_Z + 18496)
        kc2 = at("mem_k_cache", [P, NS, 2, NP], R_YH)
        vc2 = at("mem_v_cache", [P, NS, 2, NP], R_M)
        o_hi = at("x_o_hi", [P, 8, T], R_YL, F32R)
        o_lo = at("x_o_lo", [P, 8, T], R_YL + 8 * TB, F32R)
        ssx = at("x_scores_sample", [NS, NP], R_YH + 20480)
        qtok = at("xq_sample_tokens", [NS, NP], R_YH + 21504)
        xsct = at("x_scores_sample_slots", [P, 2, NS], R_YH + 22528)
        xps = at("x_probs_sample", [P, 2, NS], R_YH + 22592)
        xst = at("x_softmax_stats", [P, 8], R_YH + 22656)
        xss = at("x_softmax_stats_sample", [NS, 4], R_YH + 22688)

        hrows = at("conv_history_rows", [2 * FT, 2 * NS, P], R_YH)
        hist = at("conv_history", [P, 2 * NS, 2 * FT], R_Z)
        unew = at("conv_new", [P, 2 * FT, 10], R_Z + 5632)
        cg = at("ffn_gate", [P, 3, T], R_Z + 9152)
        cv = at("ffn_value", [P, 3, T], R_Z + 9152 + 3 * TB)
        newtok = at("conv_new_rows", [2 * FT, 10, P], R_Z + 9152)
        ytok = at("y_tokens", [P, 2, D], R_HH)
        ytok_s = at("y_tokens_sample", [NS, D], R_HL)

        bank = [ctx.enter_context(nc.psum_tensor(f"bank{b}", [P, 512], F32)) for b in range(8)]

        d_toep = nc.dram_tensor("scratch_bias", [3, 8, 384], F32, kind="Internal").ap()
        d_sbias = nc.dram_tensor("scratch_sample_bias", [8, 324], F32, kind="Internal").ap()
        d_vs = nc.dram_tensor("scratch_gla_v", [4, NS, 512], F32, kind="Internal").ap()
        d_btab = nc.dram_tensor("scratch_bias_table", [3, 8, P, NP], F32, kind="Internal").ap()
        d_q = nc.dram_tensor("scratch_dil_q", [8, 3, NS, E], F32, kind="Internal").ap()

        GATE_BANKS = [0, 1, 2, 0]
        PAIR_BANKS = [1, 2, 0, 1, 2, 0, 2, 0]

        slot_loaded = [sem(f"slot{r}_loaded") for r in range(RING)]
        hi_ready = sem("weights_hi_ready")
        lo_ready = sem("weights_lo_ready")
        projected = sem("slots_projected")
        evac = [sem(f"bank{b}_emptied") for b in range(3)]
        book = {"c": 0, "bank": {0: 0, 1: 0, 2: 0}, "evac": evac}
        PH_GA = Phase(book, 1, [0], 1)
        PH_GLA = Phase(book, 12, [1, 2, 0] * 4, 4)
        PH_GLA_G = Phase(book, 3, [2, 1, 0], 1)
        PH_GLA_B = Phase(book, 6, [1, 2, 0, 1, 2, 0], 4)
        PH_GLA_E = Phase(book, 5, [1, 2, 0, 1, 2], 1)
        PH_DIL = Phase(book, 9, [0, 1, 2] * 3, 8)
        PH_DIL_G = Phase(book, 4, GATE_BANKS, 1)
        PH_DIL_B = Phase(book, 6, PAIR_BANKS, 3)
        PH_DIL_E = Phase(book, 2, [1, 2, 0, 1], 1)
        PH_PU = Phase(book, 8, [0, 1, 2, 0, 1, 2, 0, 1], 1)
        PH_PL_G = Phase(book, 4, GATE_BANKS, 1)
        PH_PW = Phase(book, 1, [1, 2, 0, 1, 2, 0, 1, 2], 1)
        PH_PL_B = Phase(book, 6, PAIR_BANKS, 3)
        PH_PL_E = Phase(book, 2, [1, 2, 0, 1], 1)
        THREE = [0, 1, 2]
        PH_MO = Phase(book, 3, THREE, 5)
        PH_MO_E = Phase(book, 1, [0], 1)
        PH_KV = Phase(book, 3, [1, 2, 0], 5)
        PH_KV_E = Phase(book, 1, [1], 1)
        PH_XQ = Phase(book, 8, [2, 0, 1, 2, 0, 1, 2, 0], 1)
        PH_XO = Phase(book, 3, [1, 2, 0, 1, 2, 0], 2)
        PH_XO_E = Phase(book, 2, [1, 2, 0, 1], 1)
        PH_FFN = []
        for half in range(2):
            PH_FFN.append((Phase(book, 6, [2, 0, 1] * 2, 7), Phase(book, 2, [2, 0], 1),
                           Phase(book, 6, [1, 2, 0], 5), Phase(book, 2, [1], 1)))
        SLOTS = book["c"]

        TAIL_SEQS = [(0,), (1,), (2, 3), (4, 5), (6, 7)]

        counted = []

        def steps(name, names):
            counted.append(Steps(sem(name), names))
            return counted[-1]

        A_SET = steps("scalar_setup", "sq0 sq2 root sx0 sx2 " + " ".join(f"hi{t}" for t in range(KB)))
        V_SET = steps("vector_setup", "sq1 var rstd sx1 par " + " ".join(f"lo{t}" for t in range(KB)) + " tz0 tz1 tz2 sb")
        P_SET = steps("tensor_setup", "par " + " ".join(f"x{t}" for t in range(KB)) + " tz0 tz1 tz2 sb")
        G_SET = steps("gpsimd_setup", "ident0 ident ones neg stat keep1 keep apart")
        A_PRE = steps("scalar_gate", "abs exp ln ea")
        V_PRE = steps("vector_gate", " ".join(f"z{t}" for t in range(8)) + " min scale "
                      + " ".join(f"scan{t}" for t in range(8)))
        P_PRE = steps("tensor_gate", " ".join(f"z{t}" for t in range(8)))
        G_PRE = steps("gpsimd_gate", "at0")
        A_GLA = steps("scalar_gla", "exp_q exp_k " + " ".join(f"exp_h{n}" for n in range(8))
                      + " dec at0 at1 at2 at3 vs o0 o1")
        V_GLA = steps("vector_gla", "qs0 qs1 kh0 ks0 kh1 ks1 khtok vtok0 vtok1 S0_0 S0_1 S1_0 S1_1 S2_0 S2_1 S3_0 S3_1")
        P_GLA = steps("tensor_gla", "t_kh a t_v0 t_v1 t_vs o0a u0 o1a i1 u1 i2 u2 i3 u3")
        G_GLA = steps("gpsimd_gla", "mask")
        A_GT = steps("scalar_gla_tail", " ".join(f"sd{b}_{t}" for b in range(NS) for t in range(2))
                     + " om os sq root yh0 yh1 yh2 yh3")
        V_GT = steps("vector_gla_tail", "qm " + " ".join(f"sn{b}_{t}" for b in range(NS) for t in range(2))
                     + " var rstd on osr yl0 yl1 yl2 yl3")
        P_GT = steps("tensor_gla_tail", " ".join(f"os{b}" for b in range(NS)) + " ot ssq")

        A_DIL = steps("scalar_dil", "kv0 kv1 e1 e0")
        V_DIL = steps("vector_dil", "b1_0 b0_0 qk0 b1_1 b0_1 m0 sc0 b1_2 b0_2 qk1 mx1 mx0 rc n1 n0")
        P_DIL = steps("tensor_dil", "s_0 kv0 qs0 s_1 s_2 kv1 qs1")
        G_DIL = steps("gpsimd_dil", "st0 st1")
        A_DT = steps("scalar_dil_tail", "kv2 pt0 pt2 yh se ps0 ps1 yhs")
        V_DT = steps("vector_dil_tail", "qk2 pt1 m1 sc1 yl nw0 nw1 nw2 vn m2 sc2 sb sbn smx src sn dg0 dg1 dg2 yls")
        P_DT = steps("tensor_dil_tail", "kv2 qs2 pt0 pt1 pt2 pv sct pst pvs")
        G_DT = steps("gpsimd_dil_tail", "st2")
        V_DB = steps("vector_dil_branch", "add0 add1 add2 add3")
        V_DE = steps("vector_dil_branch_end", "add0 add1 add2 add3")
        A_PO = steps("scalar_pool", "h0 d0 h1 d1 h2 d2 h3 d3 " + " ".join(f"y{t}" for t in range(8)))
        V_PO = steps("vector_pool", "pos cinv " + " ".join(
            (f"l{g - 1} ua{g - 1} ub{g - 1} " if g else "") + " ".join(f"w{g}_{k}" for k in range(g + 1))
            + f" f{g} dp{g} ds{g}" for g in range(4)) + " l3 ua3 ub3")
        P_PO = steps("tensor_pool", "h0 h1 o0 h2 o1 h3 o2 " + " ".join(f"w{t}" for t in range(7)) + " o3")
        G_PO = steps("gpsimd_pool", "zero")
        V_PB = steps("vector_pool_branch", "add0 add1 add2 add3")
        V_PE = steps("vector_pool_branch_end", "add0 add1 add2 add3")
        ph_in = sem("pool_history_loaded")
        po_out = sem("pool_rows_stored")
        A_MH = steps("scalar_merged", "m0 m1 m2 m3")
        V_MH = steps("vector_merged", "m0 m1 m2 m3 zero")
        A_MM = steps("scalar_memory", "s0 s1 root x0 x1 " + " ".join(f"hi{t}" for t in range(KB)))
        V_MM = steps("vector_memory", "var rstd " + " ".join(f"lo{t}" for t in range(KB)))
        P_MM = steps("tensor_memory", " ".join(f"x{t}" for t in range(KB)))
        mem_in = sem("memory_loaded")
        x2_in = sem("x_loaded_again")
        V_OUT = {"mix": steps("vector_mix_out", "acc0 acc1 acc2"), "mix_end": steps("vector_mix_out_end", "acc0"),
                 "xo": steps("vector_xo", " ".join(f"acc{k}" for k in range(6))),
                 "xo_end": steps("vector_xo_end", "acc0 acc1 acc2 acc3"),
                 "down": steps("vector_down", "acc0 acc1 acc2"), "down_end": steps("vector_down_end", "acc0")}
        A_OUT = {"down": steps("scalar_down", "sq0 sq1 sq2"), "down_end": steps("scalar_down_end", "sq0")}
        A_N, V_N, P_N = [], [], []
        for n in range(3):
            tiles = range(KB)
            A_N.append(steps(f"scalar_norm{n}", "root" + (" " + " ".join(f"q{t}" for t in tiles) +
                " root2 " + " ".join(f"hi{t}" for t in tiles) if n < 2 else "")))
            lo = [" ".join(f"lo{4 * c + t}" for t in range(4)) for c in range(4)]
            V_N.append(steps(f"vector_norm{n}", "var rstd " + " ".join(
                f"yr{c} " + " ".join(f"x{4 * c + t}" for t in range(4)) for c in range(4)) + (
                f" var2 rstd2 t0 t1 {lo[0]} t2 {lo[1]} t3 {lo[2]} {lo[3]} zero" if n == 1 else
                " var2 rstd2 " + " ".join(f"t{c} {lo[c]}" for c in range(4)) + " zero" if n == 0 else "")))
            P_N.append(steps(f"tensor_norm{n}", "sum " + (" ".join(f"xt{t}" for t in tiles) + " " if n == 0 else "")
                             + (" ".join(f"s{t}" for t in tiles) if n < 2 else "")))
        V_KK = steps("vector_mem_k", "k0 k1 k2")
        V_KV = steps("vector_mem_kv", "t0 t1 t2")
        P_KV = steps("tensor_mem_kv", "t0 t1 t2")
        V_KE = steps("vector_mem_kv_end", "t0")
        P_KE = steps("tensor_mem_kv_end", "t0")
        mem_out = [sem("mem_k_stored"), sem("mem_v_stored")]
        X_PIECES = 6
        X_ORDER = [[(s - 2 - 2 * h, h) for h in range(4) if 0 <= s - 2 - 2 * h < X_PIECES] for s in range(8 + X_PIECES)]

        def x_names(pieces):
            return " ".join(f"{n}_{h}" for slot in X_ORDER for p, h in slot for n in pieces[p].split())
        P_X = steps("tensor_x", x_names(["sc qs", "pt sp0 sp1", "o sp2 sp3", "sct", "ps", "pv"]))
        A_X = steps("scalar_x", x_names(["qt e0 e1", "pt", "oh", "se", "ps", "ohs"]))
        V_X = steps("vector_x", x_names(["mx mxs rc n0 n1", "k0 k1 k2 k3", "ol k4 k5 k6 k7", "smx smxs src sn", "", "ols"]))
        kc_in = [sem("mem_k_cache_first_loaded"), sem("mem_k_cache_second_loaded")]
        vc_in = sem("mem_v_cache_loaded")
        hr_in = sem("conv_history_loaded")
        P_H = steps("tensor_conv_history", "h0 h1 h2 h3")
        V_H = steps("vector_conv_history", "h0 h1 h2 h3")
        A_F, V_F, A_FE, V_FE = [], [], [], []
        for half in range(2):
            A_F.append(steps(f"scalar_ffn{half}", " ".join(f"c{2 * q} n{2 * q} g{q} c{2 * q + 1} n{2 * q + 1} hi{q}"
                                                        for q in range(3))))
            V_F.append(steps(f"vector_ffn{half}", " ".join(
                f"s{2 * q} r{2 * q} w{2 * q} s{2 * q + 1} r{2 * q + 1} w{2 * q + 1} m{q} lo{q}" for q in range(3))))
            A_FE.append(steps(f"scalar_ffn{half}_end", "c0 n0 g0 c1 n1 hi0"))
            V_FE.append(steps(f"vector_ffn{half}_end", "s0 r0 w0 s1 r1 w1 m0 lo0"))
        P_Y = steps("tensor_y", "c0 c1 c2 c3 c4 " + " ".join(f"y{c}" for c in range(4)))
        A_Y = steps("scalar_y", " ".join(f"y{c} z{c}" for c in range(4)))
        V_Y = steps("vector_y", "c0 c1 c2 c3 c4 " + " ".join(f"y{c}" for c in range(4)))
        y_out = sem("y_stored")
        conv_out = sem("conv_rows_stored")
        bt_made = sem("bias_tables_made")
        bt_in = sem("bias_table_loaded")
        dq_st = sem("dil_q_stored")
        bs_in = sem("bias_sample_loaded")
        k_in = sem("k_cache_loaded")
        k2_in = sem("k_cache_third_group_loaded")
        v_in = sem("v_cache_loaded")
        qb_in = sem("q_spread_loaded")
        kv_st = [sem(f"kv{g}_stored") for g in range(3)]
        qs_st = [sem(f"qkv_sample{g}_stored") for g in range(3)]
        gpsimd_turns = sem("gpsimd_turns")
        sp_turns = sem("sp_turns")
        x_loaded = sem("x_loaded")
        par_loaded = sem("parameters_loaded")
        bias_loaded = sem("bias_inputs_loaded")
        a2_loaded = sem("w_a2_loaded")
        bias_stored = sem("bias_stored")
        vs_stored = sem("gla_v_sample_stored")
        S_stored = sem("gla_state_stored")
        ss_in = [sem(f"gla_sample_state{r}_loaded") for r in range(2)]
        ss_out = [sem(f"gla_sample_state{r}_stored") for r in range(2)]
        vb_in = [sem(f"gla_v_spread{r}_loaded") for r in range(2)]
        credits = [(lo_ready, RING)] + [(s, 1) for s in evac]
        credits += [(s.sem, s.n) for s in counted]

        def split_hi(act, p, j, i=0, ahead=RING):
            r = p.s(j + ahead)
            act.wait_ge(projected, p.c(j, i) + 1)
            act.wait_ge(slot_loaded[r], (p.third(j, i) + 2) * 16)
            nc.scalar.activation(w_hi[:, r, :], raw[:, r, :], ACT.Copy).then_inc(hi_ready, 1)

        def split_lo(dve, p, j, i=0, ahead=RING):
            r = p.s(j + ahead)
            dve.wait_ge(hi_ready, p.c(j, i) + RING + 1)
            dve.wait_ge(projected, p.c(j, i) + 1)
            nc.vector.tensor_tensor(w_lo[:, r, :], raw[:, r, :], w_hi[:, r, :].bitcast(F32),
                                    ALU.subtract).then_inc(lo_ready, 1)

        def load(sp, p, j, i, parts):
            sp.wait_ge(lo_ready, p.c(j, i) + 1)
            r = p.s(j)
            for b0, nb, width, src in parts:
                sp.dma_start(raw[:, r, b0 * P:b0 * P + nb * width].rearrange("p (k n) -> p k n", n=width),
                             src.rearrange("(k p) n -> p k n", p=P)).then_inc(slot_loaded[r], 16)

        def product(pe, p, j, k, i, blocks, last=True, first=True, fresh=True, cols=T, each=None):
            if fresh:
                pe.wait_ge(lo_ready, p.c(j, i) + RING + 1)
            r, out = p.s(j), bank[p.outs[k]][:, 0:cols]
            if first:
                pe.wait_ge(*p.freed(k, i))
            for n, (off, xh, xl) in enumerate(blocks):
                wh, wl = w_hi[:, r, off:off + P], w_lo[:, r, off:off + P]
                if each:
                    pe.wait_ge(*each(n))
                nc.tensor.matmul(out, wh, xh, start=first and n == 0, stop=False)
                nc.tensor.matmul(out, wh, xl, start=False, stop=False)
                mm = nc.tensor.matmul(out, wl, xh, start=False, stop=last and n == len(blocks) - 1)
            return mm

        def more(p, j, i):
            return not isinstance(i, int) or p.c(j, i) + RING < SLOTS

        def over(x_hi, x_lo, n=KB, off=0, b0=0, width=P):
            return [(off + k * width, x_hi[:, b0 + k, :], x_lo[:, b0 + k, :]) for k in range(n)]

        def turn(out, in_, rows):
            return nc.tensor.transpose(out, in_, ident[0:rows, 0:rows])

        w_in = A["w_in"][0]

        def w_cols(col):
            return [(0, KB, P, w_in[:, ds(col, P)])]

        def param(first, idx=0, rows=P):
            return par[0:rows, ds(idx + first, 1)]

        def wait_loop(pool, *waits):
            for s, value in waits:
                pool.wait_ge(s, value)
            pool.sem_inc(gpsimd_turns, 1)

        def wait_here(sp, *waits):
            for s, value in waits:
                sp.wait_ge(s, value)
            sp.sem_inc(sp_turns, 1)

        caches = [A[f"cache_dil{g + 1}_kv"][0] for g in range(3)]

        def cache_rows(g, kv, h):
            n = DSLOTS[g]
            return caches[g][:, 0:CACHE[g]:DILS[g], kv, ds(h, 1), :].rearrange("b s a e -> s b (a e)"), n

        mem_cache = A["cache_mem_kv"][0].rearrange("b (m p) v h e -> v h p b m e", p=P)

        block = ctx.enter_context(nc.Block())

        @block.sync
        def _(sp):
            for m in range(2):
                sp.dma_start(xtok[:, m, :], A["x_prompt"][0, m * P:(m + 1) * P, :]).then_inc(x_loaded, 16)
            sp.dma_start(xtok_s[:, :], A["x_sample"][:, 0, :]).then_inc(x_loaded, 16)
            sp.wait_ge(x_loaded, 48)
            load(sp, PH_GA, 0, 0, w_cols(COL_GA))
            with sp.Fori(0, 4) as h:
                for j in range(12):
                    kind, t = [("q", 0), ("q", 1), ("k", 0), ("k", 1)][j] if j < 4 else ("vr"[j // 8], j % 4)
                    col = {"q": h * 256 + COL_GQ, "k": h * 256 + COL_GK, "v": h * 512 + COL_GV,
                           "r": h * 512 + COL_GR}[kind]
                    load(sp, PH_GLA, j, h, w_cols(col + t * P))
            def gate_src(branch, n):
                return w_cols(n * P + (COL_GATE + branch * D))

            def bg_src(n):
                return [(0, KB, P, A["w_br_gla"][0][:, ds(n * P, P)])]
            for j in range(3):
                load(sp, PH_GLA_G, j, 0, gate_src(2, j))
            with sp.Fori(0, 4) as i:
                for j in range(3):
                    load(sp, PH_GLA_B, 2 * j, i, bg_src(i * 3 + j))
                    load(sp, PH_GLA_B, 2 * j + 1, i, gate_src(2, i * 3 + (j + 3)))
            for j, src in enumerate([bg_src(12), gate_src(2, 15), bg_src(13), bg_src(14), bg_src(15)]):
                load(sp, PH_GLA_E, j, 0, src)

            def pair_src(w, i):
                return [(0, 8, 2 * P, w[:, ds(i * 2 * P, 2 * P)])]

            def k_load(h, g):
                wait_here(sp, V_DT.at("sc2", h - 1) if g == 0 else V_DIL.at("sc0", h))
                src, n = cache_rows(g, 0, h)
                sp.dma_start(kcache[0:n, :, :], src).then_inc(k_in, 16)

            def v_load(h):
                wait_here(sp, P_DT.at("pvs", h - 1))
                for g in range(3):
                    src, n = cache_rows(g, 1, h)
                    sp.dma_start(vcache[0:n, g, :, :], src).then_inc(v_in, 16)

            def bias_load(h):
                wait_here(sp, V_DIL.at("b0_2", h - 1))
                sp.dma_start(btab[:, :, :], d_btab[:, ds(h, 1)].rearrange("g a q k -> q (g a) k")).then_inc(bt_in, 16)

            def dil_loads(h, first):
                for j in range(9):
                    if not first:
                        if j == 2:
                            k_load(h - 1, 1)
                        if j == 3:
                            v_load(h - 1)
                    if j == 5:
                        if first:
                            sp.wait_ge(bt_made, 48)
                            sp.wait_ge(projected, PH_DIL.c(0))
                        bias_load(h)
                    load(sp, PH_DIL, j, h, w_cols(h * E + (COL_DIL + 3 * DIL_W * (j // 3) + DIL_W * (j % 3))))
                    if j == 8:
                        k_load(h, 0)
            dil_loads(0, True)
            with sp.Fori(1, 8) as h:
                dil_loads(h, False)

            def pair_branch_loads(p_g, p_b, p_e, branch, w, between):
                for j in range(4):
                    load(sp, p_g, j, 0, gate_src(branch, j))
                    between(j)
                with sp.Fori(0, 3) as i:
                    for q in range(2):
                        load(sp, p_b, 3 * q, i, pair_src(w, i * 2 + q))
                        for r in range(2):
                            load(sp, p_b, 3 * q + 1 + r, i, gate_src(branch, i * 4 + (4 + 2 * q + r)))
                for q in range(2):
                    load(sp, p_e, q, 0, pair_src(w, 6 + q))

            def dil_last(j):
                if j == 1:
                    k_load(7, 1)
                if j == 2:
                    v_load(7)
            pair_branch_loads(PH_DIL_G, PH_DIL_B, PH_DIL_E, 1, A["w_br_dil"][0], dil_last)
            sp.wait_ge(*G_DT.at("st2", 7))
            sp.wait_ge(*P_DT.at("pvs", 7))
            sp.dma_start(ptok[:, :], A["state_pool"][0].rearrange("b r c -> (b r) c")).then_inc(ph_in, 16)
            for j in range(8):
                load(sp, PH_PU, j, 0, w_cols(COL_POOL + j * P))

            def pool_load(j):
                if j == 3:
                    load(sp, PH_PW, 0, 0, [(0, 8, 2 * P, A["pool_w"][0].rearrange("g c d -> (g c) d"))])
            pair_branch_loads(PH_PL_G, PH_PL_B, PH_PL_E, 0, A["w_br_pool"][0], pool_load)
            sp.wait_ge(*V_PO.at("l3"))
            sp.wait_ge(*P_PO.at("o3"))
            for m in range(2):
                sp.dma_start(memtok[:, m, :], A["mem_prompt"][0, m * P:(m + 1) * P, :]).then_inc(mem_in, 16)

            def wide(w, n):
                return [(0, KB, P, w[:, ds(n * P, P)])]

            for j in range(3):
                load(sp, PH_MO, j, 0, wide(A["w_mix_out"][0], j))
            with sp.Fori(1, 3) as i:
                for j in range(3):
                    load(sp, PH_MO, j, i, wide(A["w_mix_out"][0], i * 3 + j))
            sp.wait_ge(*V_PE.at("add3"))
            sp.wait_ge(po_out, 48)
            for m in range(2):
                sp.dma_start(xtok2[:, m, :], A["x_prompt"][0, m * P:(m + 1) * P, :]).then_inc(x2_in, 16)
                sp.dma_start(xtok2_s[m][:, :], A["x_sample"][:, 0, m * 1024:(m + 1) * 1024]).then_inc(x2_in, 16)
            with sp.Fori(3, 5) as i:
                for j in range(3):
                    load(sp, PH_MO, j, i, wide(A["w_mix_out"][0], i * 3 + j))
            load(sp, PH_MO_E, 0, 0, wide(A["w_mix_out"][0], 15))
            with sp.Fori(0, 5) as i:
                for j in range(3):
                    load(sp, PH_KV, j, i, wide(A["w_xkv"][0], i * 3 + j))
            load(sp, PH_KV_E, 0, 0, wide(A["w_xkv"][0], 15))
            for j in range(8):
                load(sp, PH_XQ, j, 0, wide(A["w_xq"][0], j))
            with sp.Fori(0, 2) as i:
                for j in range(3):
                    load(sp, PH_XO, j, i, pair_src(A["w_xo"][0], i * 3 + j))
            for j in range(2):
                load(sp, PH_XO_E, j, 0, pair_src(A["w_xo"][0], 6 + j))
            for half, (up, up_e, down, down_e) in enumerate(PH_FFN):
                def up_src(n, kind):
                    return wide(A["w_up"][0], n + (half * FH + kind * FT))

                def down_src(n, part):
                    r0 = (half * FH + part * (FH // 2)) * P
                    return [(0, FH // 2, P, A["w_down"][0][r0:r0 + FH // 2 * P, ds(n * P, P)])]
                with sp.Fori(0, 7) as i:
                    for j in range(6):
                        load(sp, up, j, i, up_src(i * 3 + j // 2, j % 2))
                for j in range(2):
                    load(sp, up_e, j, 0, up_src(21, j))
                with sp.Fori(0, 5) as i:
                    for j in range(6):
                        load(sp, down, j, i, down_src(i * 3 + j // 2, j % 2))
                for j in range(2):
                    load(sp, down_e, j, 0, down_src(15, j))
            for c in range(4):
                sp.wait_ge(*V_Y.at(f"y{c}"))
                sp.wait_ge(*A_Y.at(f"z{c}"))
                cols = slice(c * 512, c * 512 + 512)
                sp.dma_start(A["y_p"][0].rearrange("(m p) d -> p m d", p=P)[:, :, cols], ytok[:, :, cols])\
                    .then_inc(y_out, 16)
                sp.dma_start(A["y_s"][:, 0, cols], ytok_s[:, cols]).then_inc(y_out, 16)
            sp.wait_ge(y_out, 8 * 16)

        @block.gpsimd
        def _(pool):
            for s, n in credits:
                pool.sem_inc(s, n)
            nc.gpsimd.memset(ident[:, :], 0.0).then_inc(G_SET("ident0"), 1)
            pool.wait_ge(*G_SET.at("ident0"))
            nc.gpsimd.affine_select(out=ident[:, :], in_=ident[:, :], compare_op=ALU.not_equal, fill=1.0, base=0,
                                    pattern=[[-1, P]], channel_multiplier=1).then_inc(G_SET("ident"), 1)
            nc.gpsimd.memset(ones[:, :], 1.0).then_inc(G_SET("ones"), 1)
            pool.wait_ge(*G_SET.at("ones"))
            nc.gpsimd.memset(relx[32:33, :], NEG).then_inc(G_SET("neg"), 1)
            pool.wait_ge(*G_SET.at("neg"))
            nc.gpsimd.memset(stat[:, :], 1.0).then_inc(G_SET("stat"), 1)
            nc.gpsimd.memset(scan_keep[:, :], 1.0).then_inc(G_SET("keep1"), 1)
            pool.wait_ge(*G_SET.at("keep1"))
            nc.gpsimd.memset(scan_keep[:, 0:NP:64], 0.0).then_inc(G_SET("keep"), 1)
            nc.gpsimd.memset(g_qm[:, :, :, :], 0.0).then_inc(G_SET("apart"), 1)
            pool.wait_ge(*V_SET.at("tz2"))
            pool.dma_start(d_toep[:, :, 0:383].rearrange("g h d -> h g d"), toep[:, :, 0:383]).then_inc(bias_stored, 16)
            pool.wait_ge(*V_SET.at("sb"))
            pool.dma_start(d_sbias[:, 0:SSEEN + 3], sbias_all[:, 0:SSEEN + 3]).then_inc(bias_stored, 16)
            pool.wait_ge(bias_stored, 32)
            pool.wait_ge(*V_PRE.at("scan7"))
            nc.gpsimd.memset(g_at[:, :, :], 0.0).then_inc(G_PRE("at0"), 1)

            def gla_head(h):
                wait_loop(pool, A_GLA.at("at3", h))
                nc.gpsimd.affine_select(out=g_at[:, :, :], in_=g_at[:, :, :], compare_op=ALU.is_ge, fill=0.0, base=0,
                                        pattern=[[0, 2], [1, P]], channel_multiplier=-1).then_inc(G_GLA("mask"), 1)
                if not isinstance(h, int):
                    for r in range(2):
                        wait_loop(pool, (ss_out[r], h * 64))
                wait_loop(pool, A_GLA.at("vs", h))
                pool.dma_start(d_vs[ds(h, 1)].rearrange("a b v -> (a b) v"), g_vs[:, :]).then_inc(vs_stored, 16)
                wait_loop(pool, V_GLA.at("S3_1", h))
                pool.dma_start(A["gla_p"][0, 0][ds(h, 1)].rearrange("a (t p) v -> p (a t) v", p=P),
                               g_S[:, :, :]).then_inc(S_stored, 16)

            def states(name, h, b):
                return A[name][0, b][ds(h, 1)].rearrange("a (t p) v -> p (a t) v", p=P)

            def ss_load(h, q):
                r = q % 2
                if q < 2:
                    wait_loop(pool, P_GT.at(f"os{2 * q + 5}", h - 1), (vs_stored, h * 16 + 16))
                else:
                    wait_loop(pool, P_GT.at(f"os{2 * q - 3}", h), (ss_out[r], h * 64 + 32))
                for b in (2 * q, 2 * q + 1):
                    pool.dma_start(g_Ss[b % 4][:, :, :], states("state_gla", h, b)).then_inc(ss_in[r], 16)
                rows = d_vs[ds(h, 1), 2 * q:2 * q + 2, :].rearrange("a b v -> a (b v)")
                pool.dma_start(g_vb[:, 2 * r:2 * r + 2, :].rearrange("p b v -> p (b v)"),
                               rows.to_broadcast([P, 1024])).then_inc(vb_in[r], 16)

            def gla_tail(h):
                for q in range(2):
                    ss_load(h, q)
                for q in range(4):
                    wait_loop(pool, V_GT.at(f"sn{2 * q + 1}_1", h))
                    for b in (2 * q, 2 * q + 1):
                        pool.dma_start(states("gla_s", h, b), g_Ss[b % 4][:, :, :]).then_inc(ss_out[q % 2], 16)
                    if q < 2:
                        ss_load(h, q + 2)

            gla_head(0)
            with pool.Fori(1, 4) as h:
                gla_tail(h - 1)
                gla_head(h)
            gla_tail(3)
            for r in range(2):
                pool.wait_ge(ss_out[r], 4 * 64)
            pool.wait_ge(S_stored, 4 * 16)

            def dil_group(h, g, step):
                new = A[f"dil{g + 1}_s"][0]
                wait_loop(pool, (V_DT if g == 2 else V_DIL).at(f"qk{g}", h))
                pool.dma_start(d_q[ds(h, 1), g].rearrange("a b e -> (a b) e"), qkvs[:, g, 0:E]).then_inc(dq_st, 16)
                wait_loop(pool, (dq_st, h * 48 + (16 * g + 16)), V_DT.at("m2", h - 1) if g == 0
                          else V_DIL.at("m0", h) if g == 1 else V_DT.at("m1", h))
                row = d_q[ds(h, 1), g].rearrange("a b e -> a (b e)")
                pool.dma_start(qspread[:, :, :].rearrange("p b e -> p (b e)"), row.to_broadcast([P, NS * E]))\
                    .then_inc(qb_in, 16)
                wait_loop(pool, (A_DT if g == 2 else A_DIL).at(f"kv{g}", h))
                dst_p = A[f"dil{g + 1}_p"][0, 0]
                for m in range(2):
                    if g or m:
                        t0 = m * P if g else 0
                        pool.dma_start(dst_p[t0:t0 + P, :, ds(h, 1), :].rearrange("t v a e -> t v (a e)"),
                                       kvtok[:, g, :, m, :]).then_inc(kv_st[g], 16)
                pool.dma_start(new[:, 0, :, ds(h, 1), :].rearrange("b v a e -> b v (a e)"),
                               qkvs[:, g, E:3 * E].rearrange("b (v e) -> b v e", e=E)).then_inc(qs_st[g], 16)
                for s, v in ((kv_st[g], h * (32 if g else 16) + (32 if g else 16)), (qs_st[g], h * 16 + 16)):
                    pool.wait_ge(s, v)
                pool.sem_inc(step, 1)

            def dil_body(h):
                dil_group(h, 0, G_DIL("st0"))
                dil_group(h, 1, G_DIL("st1"))

            def dil_tail(h):
                dil_group(h, 2, G_DT("st2"))
                wait_loop(pool, V_DT.at("sbn", h - 1))
                pool.dma_start(bsamp[:, 0:SSEEN + 3], d_sbias[ds(h, 1), 0:SSEEN + 3].to_broadcast([NS, SSEEN + 3]))\
                    .then_inc(bs_in, 16)
            dil_body(0)
            with pool.Fori(1, 8) as h:
                dil_tail(h - 1)
                dil_body(h)
            dil_tail(7)
            pool.wait_ge(*P_DT.at("pvs", 7))
            nc.gpsimd.memset(u_ctx[:, :, 0:UP], 0.0)
            nc.gpsimd.memset(u_ctx[:, :, US - 1:US], 0.0).then_inc(G_PO("zero"), 1)
            pool.dma_start(A["pool_s"][0][:, 0:14, :], A["state_pool"][0][:, 1:15, :]).then_inc(po_out, 16)
            pool.wait_ge(*V_PO.at("ub3"))
            pool.dma_start(A["pool_p"][0, 0], utok[:, :]).then_inc(po_out, 16)
            pool.dma_start(A["pool_s"][0][:, 14, :], utok_s[:, :]).then_inc(po_out, 16)
            pool.wait_ge(po_out, 48)
            pool.wait_ge(*V_KV.at("t1", 2))
            pool.dma_start(A["mem_p"][0, 0].rearrange("(m p) v h e -> p v m (h e)", p=P)[:, 0], kvtok2[:, 0, :, :])\
                .then_inc(mem_out[0], 16)

            def k_half(h, half):
                for b in range(4 * half, 4 * half + 4):
                    pool.dma_start(kc2[:, b, :, :], mem_cache[0, h, :, b]).then_inc(kc_in[half], 16)
            pool.wait_ge(projected, PH_KV_E.c(0) + 1)
            for half in range(2):
                k_half(0, half)
            pool.wait_ge(*V_KE.at("t0"))
            pool.dma_start(A["mem_p"][0, 0].rearrange("(m p) v h e -> p v m (h e)", p=P)[:, 1], kvtok2[:, 1, :, :])\
                .then_inc(mem_out[1], 16)
            for h in range(1, 4):
                for half in range(2):
                    pool.wait_ge(*V_X.at(f"k{4 * half + 3}_{h - 1}"))
                    k_half(h, half)
            pool.wait_ge(*V_X.at("k7_3"))
            states = A["state_ffn_conv"][0].rearrange("b r (t p) -> (b r) t p", p=P)
            pool.dma_start(hrows[:, :, :], states.rearrange("a t p -> t a p")).then_inc(hr_in, 16)
            pool.dma_start(A["conv_s"][0][:, 0, :], A["state_ffn_conv"][0][:, 1, :]).then_inc(conv_out, 16)
            pool.wait_ge(mem_out[1], 16)
            pool.wait_ge(*V_Y.at("c4"))
            pool.dma_start(A["conv_p"][0, 0].rearrange("r (t p) -> t r p", p=P), newtok[:, 0:2, :]).then_inc(conv_out, 16)
            pool.dma_start(A["conv_s"][0][:, 1, :].rearrange("b (t p) -> t b p", p=P), newtok[:, 2:10, :])\
                .then_inc(conv_out, 16)
            pool.wait_ge(conv_out, 48)

        @block.scalar
        def _(act):
            groups = [("norm_mix_pre", 0), ("norm_mix_post", 16), ("norm_x_pre", 32), ("norm_x_post", 48),
                      ("norm_mem", 64), ("norm_ffn_pre", 80), ("norm_ffn_post", 96), ("pool_scale", 112),
                      ("gla_b_a", 120)]
            for name, r0 in groups:
                src = A[name].rearrange("l (t p) -> (l t) p", p=P)
                act.dma_start(prow[r0:r0 + src.shape[0], 0, :], src).then_inc(par_loaded, 16)
            act.dma_start(prow[0:16, 1, :], A["gla_norm"].rearrange("l (t p) -> (l t) p", p=P)).then_inc(par_loaded, 16)
            conv = A["conv_w"].rearrange("l i (t p) -> (l i) t p", p=P)
            act.dma_start(prow[16:104, 1, :], conv[0]).then_inc(par_loaded, 16)
            act.dma_start(prow[0:88, 2, :], conv[1]).then_inc(par_loaded, 16)
            act.dma_start(prow[0:88, 3, :], conv[2]).then_inc(par_loaded, 16)
            act.dma_start(prow[0:88, 4, :], A["conv_b"].rearrange("l (t p) -> (l t) p", p=P)).then_inc(par_loaded, 16)
            act.dma_start(onehot[:, :], A["onehot"]).then_inc(bias_loaded, 16)
            act.dma_start(relx[0:32, :], A["rel_bias"]).then_inc(bias_loaded, 16)
            act.dma_start(w_a2[:, :], A["gla_w_a2"][0]).then_inc(a2_loaded, 16)
            act.wait_ge(x_loaded, 48)
            act.wait_ge(*G_SET.at("stat"))
            ours = ((0, xtok[:, 0, :], P), (2, xtok_s[:, :], NS))
            for m, x, n in ours:
                if m:
                    act.wait_ge(*A_SET.at("sq0"))
                nc.scalar.activation(junk[0][0:n, :], x, ACT.Square, accum_out=stat[0:n, m:m + 1])\
                    .then_inc(A_SET(f"sq{m}"), 1)
            act.wait_ge(*V_SET.at("var"))
            nc.scalar.activation(stat[:, 6:9], stat[:, 3:6], ACT.Sqrt).then_inc(A_SET("root"), 1)
            act.wait_ge(*V_SET.at("rstd"))
            for m, x, n in ours:
                nc.scalar.activation(x, x, ACT.Copy, scale=stat[0:n, 9 + m:10 + m]).then_inc(A_SET(f"sx{m}"), 1)

            def first_hi(c):
                act.wait_ge(slot_loaded[c], 16)
                nc.scalar.activation(w_hi[:, c, :], raw[:, c, :], ACT.Copy).then_inc(hi_ready, 1)
            first_hi(0)
            act.wait_ge(*V_SET.at("par"))
            for t in range(KB):
                act.wait_ge(*P_SET.at(f"x{t}"))
                nc.scalar.activation(h_hi[:, t, :], bank[3 + t % 4][:, 0:T], ACT.Copy,
                                     scale=param(PC_MIXPRE, t)).then_inc(A_SET(f"hi{t}"), 1)
                if t in (7, 15):
                    first_hi(1 + t // 8)

            act.wait_ge(projected, PH_GA.c(0) + 1)
            act.wait_ge(*PH_GA.freed(0))
            nc.scalar.activation(ga[:, :], bank[0][0:16, 0:T], ACT.Copy).then_inc(evac[0], 1)
            split_hi(act, PH_GA, 0)
            act.wait_ge(*V_PRE.at("z7"))
            nc.scalar.activation(gtmp[:, :, :], la[:, :, :], ACT.Abs).then_inc(A_PRE("abs"), 1)
            act.wait_ge(*A_PRE.at("abs"))
            nc.scalar.activation(gtmp[:, :, :], gtmp[:, :, :], ACT.Exp, scale=-1.0).then_inc(A_PRE("exp"), 1)
            act.wait_ge(*A_PRE.at("exp"))
            nc.scalar.activation(gtmp[:, :, :], gtmp[:, :, :], ACT.Ln, bias=1.0).then_inc(A_PRE("ln"), 1)
            act.wait_ge(*V_PRE.at("scan7"))
            nc.scalar.activation(la[:, :, NP:T], la[:, :, NP:T], ACT.Exp).then_inc(A_PRE("ea"), 1)
            act.wait_ge(*A_PRE.at("ea"))
            act.wait_ge(*G_PRE.at("at0"))
            act.wait_ge(bias_stored, 32)
            for g in range(3):
                diagonals = bass.AP(tensor=d_toep.tensor, offset=g * 8 * 384 + P - 1, ap=[[384, 8], [-1, P], [1, NP]])
                act.dma_start(d_btab[g], diagonals).then_inc(bt_made, 16)

            def gla_head(h, tail):
                p = PH_GLA
                act.wait_ge(*P_GLA.at("i3", h - 1))
                act.wait_ge(*V_GLA.at("S3_1", h - 1))
                pair = la[:, ds(h * 2, 2), :]
                nc.scalar.activation(g_qt[:, :, :], pair[:, :, 0:NP], ACT.Exp).then_inc(A_GLA("exp_q"), 1)
                nc.scalar.activation(g_kt[:, :, :], pair[:, :, 0:NP], ACT.Exp, scale=-1.0).then_inc(A_GLA("exp_k"), 1)
                for n in range(8):
                    t, k = n // 4, n % 4
                    tile = la[:, ds(h * 2 + t, 1), :]
                    nc.scalar.activation(g_kh[:, t, 64 * k:64 * k + 64], tile[:, 0, 64 * k:64 * k + 64], ACT.Exp,
                                         scale=-1.0, bias=tile[:, 0, 64 * k + 63:64 * k + 64])\
                        .then_inc(A_GLA(f"exp_h{n}"), 1)
                nc.scalar.activation(g_dec[:, :, :], pair[:, :, 63:NP:64], ACT.Exp).then_inc(A_GLA("dec"), 1)
                for j in range(12):
                    act.wait_ge(projected, p.c(j, h) + 1)
                    if 4 <= j < 8:
                        nc.scalar.activation(g_vT[:, j - 4, :], bank[p.outs[j]][:, 0:T], ACT.Copy)\
                            .then_inc(evac[p.outs[j]], 1)
                    if j >= 8:
                        if j == 8:
                            act.wait_ge(*V_GT.at("osr", h - 1))
                        nc.scalar.activation(g_sr[:, j - 8, :], bank[p.outs[j]][:, 0:T], ACT.Silu)\
                            .then_inc(evac[p.outs[j]], 1)
                    split_hi(act, p, j, h)
                    tail(j)
                    if j == 5:
                        act.wait_ge(*P_GLA.at("a", h))
                        act.wait_ge(*P_GLA.at("o1a", h - 1))
                        for n in range(4):
                            m, q = n // 2, 64 * (n % 2)
                            nc.scalar.activation(g_at[q:q + 64, m, q:q + 64],
                                                 bank[4][q:q + 64, m * P + q:m * P + q + 64], ACT.Copy)\
                                .then_inc(A_GLA(f"at{n}"), 1)
                    if j == 8:
                        act.wait_ge(*P_GLA.at("t_vs", h))
                        if not isinstance(h, int):
                            act.wait_ge(vs_stored, h * 16)
                        nc.scalar.activation(g_vs[:, :], bank[5][0:NS, :], ACT.Copy).then_inc(A_GLA("vs"), 1)
                    if j == 10:
                        act.wait_ge(*P_GLA.at("i1", h))
                        nc.scalar.activation(g_o[:, :, 0:P], bank[4][:, :].rearrange("p (v c) -> p v c", c=P),
                                             ACT.Copy).then_inc(A_GLA("o0"), 1)
                    if j == 11:
                        act.wait_ge(*P_GLA.at("i3", h))
                        nc.scalar.activation(g_o[:, :, P:NP], bank[5][:, :].rearrange("p (v c) -> p v c", c=P),
                                             ACT.Copy).then_inc(A_GLA("o1"), 1)

            def gla_tail(k, h):
                if k < 5:
                    for b in TAIL_SEQS[k]:
                        act.wait_ge(ss_in[b // 2 % 2], h * 64 + (b // 4 * 32 + 32))
                        for t in range(2):
                            st = g_Ss[b % 4][:, t, :]
                            nc.scalar.activation(st, st, ACT.Copy, scale=la[:, ds(h * 2 + t, 1), NP + b])\
                                .then_inc(A_GT(f"sd{b}_{t}"), 1)
                if k == 5:
                    act.wait_ge(*P_GT.at("os7", h))
                    nc.scalar.activation(g_om[:, :], bank[5][0:NS, :], ACT.Copy).then_inc(A_GT("om"), 1)
                if k == 6:
                    act.wait_ge(*P_GT.at("ot", h))
                    nc.scalar.activation(g_o[:, :, NP:T], bank[5][:, 0:32].rearrange("p (v b) -> p v b", b=NS),
                                         ACT.Copy).then_inc(A_GT("os"), 1)
                    act.wait_ge(*A_GT.at("os", h))
                    act.wait_ge(S_stored, h * 16 + 16)
                    nc.scalar.activation(g_sq[:, :, :], g_o[:, :, :], ACT.Square).then_inc(A_GT("sq"), 1)
                if k == 7:
                    act.wait_ge(*V_GT.at("var", h))
                    nc.scalar.activation(g_var[:, :], g_var[:, :], ACT.Sqrt).then_inc(A_GT("root"), 1)
                if k == 8:
                    act.wait_ge(*V_GT.at("osr", h))
                    for v in range(4):
                        nc.scalar.activation(y_hi[:, ds(h * 4 + v, 1), :], g_o[:, v:v + 1, :], ACT.Copy,
                                             scale=param(PC_GNORM, h * 4 + v)).then_inc(A_GT(f"yh{v}"), 1)

            gla_head(0, lambda k: None)
            with act.Fori(1, 4) as h:
                gla_head(h, lambda k: gla_tail(k, h - 1))

            for j in range(3):
                p = PH_GLA_G
                act.wait_ge(projected, p.c(j) + 1)
                if j == 0:
                    act.wait_ge(*P_GLA.at("u3", 3))
                    act.wait_ge(*V_GLA.at("S3_1", 3))
                nc.scalar.activation(gates[:, j, :], bank[p.outs[j]][:, 0:T], ACT.Sigmoid).then_inc(evac[p.outs[j]], 1)
                split_hi(act, p, j)
                gla_tail(j, 3)
            for k in range(3, 9):
                gla_tail(k, 3)
            with act.Fori(0, 4) as i:
                p = PH_GLA_B
                for j in range(6):
                    act.wait_ge(projected, p.c(j, i) + 1)
                    if j % 2:
                        act.wait_ge(*p.saved(j - 1, i))
                        nc.scalar.activation(gates[:, j // 2, :], bank[p.outs[j]][:, 0:T], ACT.Sigmoid)\
                            .then_inc(evac[p.outs[j]], 1)
                    split_hi(act, p, j, i)
            p = PH_GLA_E
            for j in range(5):
                act.wait_ge(projected, p.c(j) + 1)
                if j == 1:
                    act.wait_ge(*p.saved(0))
                    nc.scalar.activation(gates[:, 0, :], bank[p.outs[1]][:, 0:T], ACT.Sigmoid).then_inc(evac[p.outs[1]], 1)
                split_hi(act, p, j)

            def copy(out, in_):
                return nc.scalar.activation(out, in_, ACT.Copy)

            def dil_body(h, tail, first=False):
                p = PH_DIL
                for j in range(9):
                    g = j // 3
                    act.wait_ge(projected, p.c(j, h) + 1)
                    if first and j == 0:
                        act.wait_ge(*PH_GLA_E.saved(4))
                    act.wait_ge(*(P_DT if g == 2 else P_DIL).at(f"qs{g}", h - 1))
                    copy(qkvT[:, j, :], bank[p.outs[j]][:, 0:T]).then_inc(evac[p.outs[j]], 1)
                    split_hi(act, p, j, h)
                    tail(j)
                    if j in (3, 8):
                        g = (3, 8).index(j)
                        act.wait_ge(*P_DIL.at(f"kv{g}", h))
                        act.wait_ge(*G_DIL.at(f"st{g}", h - 1))
                        act.wait_ge(*P_DT.at("pv", h - 1))
                        copy(kvtok[:, g, :, :, :].rearrange("p v m e -> p (v m e)"), bank[6][:, :])\
                            .then_inc(A_DIL(f"kv{g}"), 1)
                    if j == 8:
                        for n, (sc, st, mx) in enumerate(((s1, 0, "mx1"), (s0, 1, "mx0"))):
                            act.wait_ge(*V_DIL.at(mx, h))
                            flat = sc[:, :, :].rearrange("p g k -> p (g k)")
                            nc.scalar.activation(flat, flat, ACT.Exp, bias=dst[:, st:st + 1],
                                                 accum_out=dst[:, 2 + st:3 + st]).then_inc(A_DIL(("e1", "e0")[n]), 1)

            def dil_tail(k, h):
                if k == 0:
                    act.wait_ge(*P_DT.at("kv2", h))
                    act.wait_ge(*G_DT.at("st2", h - 1))
                    copy(kvtok[:, 2, :, :, :].rearrange("p v m e -> p (v m e)"), bank[6][:, :])\
                        .then_inc(A_DT("kv2"), 1)
                if k == 1:
                    for g in (0, 2):
                        act.wait_ge(*P_DT.at(f"pt{g}", h))
                        copy(pT[:, g, :], bank[3 + g][:, 0:384]).then_inc(A_DT(f"pt{g}"), 1)
                if k == 2:
                    act.wait_ge(*P_DT.at("pv", h))
                    copy(y_hi[:, ds(h, 1), 0:NP], bank[7][:, None, 0:NP]).then_inc(A_DT("yh"), 1)
                    act.wait_ge(*V_DT.at("sc1", h))
                    src, n = cache_rows(2, 0, h)
                    act.dma_start(kcache[0:n, :, :], src).then_inc(k2_in, 16)
                if k == 5:
                    act.wait_ge(*V_DT.at("smx", h))
                    nc.scalar.activation(ssamp[:, 0:SSEEN + 3], ssamp[:, 0:SSEEN + 3], ACT.Exp, bias=dss[:, 0:1],
                                         accum_out=dss[:, 1:2]).then_inc(A_DT("se"), 1)
                if k == 6:
                    act.wait_ge(*P_DT.at("pst", h))
                    copy(psT[:, 0:2, :].rearrange("p g b -> p (g b)"), bank[7][:, 0:16]).then_inc(A_DT("ps0"), 1)
                    copy(psT[0:64, 2, :], bank[7][0:64, 16:24]).then_inc(A_DT("ps1"), 1)
                if k == 7:
                    act.wait_ge(*P_DT.at("pvs", h))
                    copy(y_hi[:, ds(h, 1), NP:T], bank[7][:, None, 32:40]).then_inc(A_DT("yhs"), 1)

            dil_body(0, lambda k: None, True)
            with act.Fori(1, 8) as h:
                dil_body(h, lambda k: dil_tail(k, h - 1))

            def pair_gates(p_g, p_b, p_e, ring, tail, early=None):
                for j in range(4):
                    act.wait_ge(projected, p_g.c(j) + 1)
                    nc.scalar.activation(ring[:, j, :], bank[p_g.outs[j]][:, 0:T], ACT.Sigmoid)\
                        .then_inc(evac[p_g.outs[j]], 1)
                    split_hi(act, p_g, j)
                    tail(j)
                for k in range(4, 8):
                    tail(k)
                with act.Fori(0, 3) as i:
                    for j in range(6):
                        act.wait_ge(projected, p_b.c(j, i) + 1)
                        if j % 3:
                            q, r = j // 3, j % 3 - 1
                            k = 4 * q + 2 + r
                            act.wait_ge(*p_b.saved(4 * q + r, i))
                            nc.scalar.activation(ring[:, 2 * q + r, :], bank[p_b.outs[k]][:, 0:T], ACT.Sigmoid)\
                                .then_inc(evac[p_b.outs[k]], 1)
                        split_hi(act, p_b, j, i)
                if early:
                    early()
                for j in range(2):
                    if p_e.c(j) + RING < SLOTS:
                        split_hi(act, p_e, j)
            pair_gates(PH_DIL_G, PH_DIL_B, PH_DIL_E, gates2, lambda k: dil_tail(k, 7))

            for j in range(8):
                g = j // 2
                act.wait_ge(projected, PH_PU.c(j) + 1)
                if j == 0:
                    act.wait_ge(*G_PO.at("zero"))
                if g >= 2:
                    act.wait_ge(*V_PO.at(f"ds{g - 2}"))
                    act.wait_ge(*P_PO.at(f"o{g - 2}"))
                ps, u = bank[PH_PU.outs[j]], u_ctx[:, j % 4, :]
                copy(u[:, UP:UP + NP], ps[:, 0:NP])
                copy(u[:, US + 15:US + 16 * NS:16], ps[:, NP:T]).then_inc(evac[PH_PU.outs[j]], 1)
                split_hi(act, PH_PU, j)
                if j % 2:
                    act.wait_ge(*P_PO.at(f"h{g}"))
                    rows = u_ctx[:, 2 * (g % 2):2 * (g % 2) + 2, US:US + 16 * NS].rearrange("p t (b r) -> p t b r", r=16)
                    copy(rows[:, :, :, 0:15], bank[3 + 2 * (g % 2)][:, 0:2 * NS * 15]
                         .rearrange("p (t b r) -> p t b r", t=2, r=15)).then_inc(A_PO(f"h{g}"), 1)
                    act.wait_ge(*V_PO.at(f"ds{g}"))
                    copy(y_hi[:, 8 + 2 * g:10 + 2 * g, :], pdiff[:, :, :]).then_inc(A_PO(f"d{g}"), 1)
            def pool_scaled(k):
                if k != 4:
                    return
                for t in range(8):
                    if t < 7:
                        act.wait_ge(*P_PO.at(f"w{t}"))
                    else:
                        act.wait_ge(projected, PH_PW.c(0) + 1)
                    nc.scalar.activation(y_hi[:, t, :], bank[PH_PW.outs[t]][:, 0:T], ACT.Copy,
                                         scale=param(PC_PSCALE, t)).then_inc(A_PO(f"y{t}"), 1)
                split_hi(act, PH_PW, 0)

            def merged_hi(c):
                if c == 0:
                    act.wait_ge(projected, PH_PL_B.c(5, 2) + 1)
                act.wait_ge(*(V_PB.at("add3", 2) if c < 3 else V_PE.at("add3")))
                copy(h_hi[:, 4 * c:4 * c + 4, :], merged[:, 4 * c:4 * c + 4, :]).then_inc(A_MH(f"m{c}"), 1)

            def merged_early():
                for c in range(3):
                    merged_hi(c)
            pair_gates(PH_PL_G, PH_PL_B, PH_PL_E, gates2, pool_scaled, merged_early)
            merged_hi(3)

            def evacuate(p, j, k, i, n, acc_before):
                out = bank[p.outs[k]][:, 0:T]
                act.wait_ge(projected, p.c(j, i) + 1)
                copy(merged[:, ds(n, 1), :], out[:, None, :])
                act.wait_ge(*acc_before)
                nc.scalar.activation(sqr[:, k % 3, :], out, ACT.Square).then_inc(evac[p.outs[k]], 1)

            def mix_body(i):
                for j in range(3):
                    evacuate(PH_MO, j, j, i, i * 3 + j, V_OUT["mix"].at(f"acc{j}", i - 1))
                    split_hi(act, PH_MO, j, i)
                    if isinstance(i, int) and j < 2:
                        if j == 0:
                            act.wait_ge(projected, PH_PL_E.c(1) + 1)
                            act.wait_ge(mem_in, 32)
                        else:
                            act.wait_ge(*A_MM.at("s0"))
                        nc.scalar.activation(sqjunk[:, :], memtok[:, j, :], ACT.Square, accum_out=mstat[:, j:j + 1])\
                            .then_inc(A_MM(f"s{j}"), 1)
                    if isinstance(i, int) and j == 2:
                        act.wait_ge(*V_MM.at("var"))
                        nc.scalar.activation(mstat[:, 4:6], mstat[:, 2:4], ACT.Sqrt).then_inc(A_MM("root"), 1)
                        act.wait_ge(*V_MM.at("rstd"))
                        for m in range(2):
                            nc.scalar.activation(memtok[:, m, :], memtok[:, m, :], ACT.Copy, scale=mstat[:, 6 + m:7 + m])\
                                .then_inc(A_MM(f"x{m}"), 1)
            mix_body(0)
            with act.Fori(1, 3) as i:
                mix_body(i)
            for t in range(KB):
                act.wait_ge(*P_MM.at(f"x{t}"))
                nc.scalar.activation(hm_hi[:, t, :], bank[3 + t % 4][:, 0:NP], ACT.Copy, scale=param(PC_MEM, t))\
                    .then_inc(A_MM(f"hi{t}"), 1)
            with act.Fori(3, 5) as i:
                mix_body(i)
            evacuate(PH_MO_E, 0, 0, 0, 15, V_OUT["mix"].at("acc0", 4))
            split_hi(act, PH_MO_E, 0)

            def norm(n, g_pre):
                act.wait_ge(*V_N[n].at("var"))
                nc.scalar.activation(rstd[:, :], rstd[:, :], ACT.Sqrt).then_inc(A_N[n]("root"), 1)
                if n == 2:
                    return
                for t in range(KB):
                    act.wait_ge(*V_N[n].at(f"x{t}"))
                    if t >= 3:
                        act.wait_ge(*P_N[n].at(f"s{t - 3}"))
                    nc.scalar.activation(sqr[:, t % 3, :], xres[:, t, :], ACT.Square).then_inc(A_N[n](f"q{t}"), 1)
                act.wait_ge(*V_N[n].at("var2"))
                nc.scalar.activation(rstd[:, :], rstd[:, :], ACT.Sqrt).then_inc(A_N[n]("root2"), 1)
                if n:
                    for c in range(4):
                        normed_hi(n, g_pre, c)

            def normed_hi(n, g_pre, c):
                for t in range(4 * c, 4 * c + 4):
                    act.wait_ge(*V_N[n].at(f"t{c}"))
                    nc.scalar.activation(h_hi[:, t, :], merged[:, t, :], ACT.Copy, scale=param(g_pre, t))\
                        .then_inc(A_N[n](f"hi{t}"), 1)
            norm(0, PC_XPRE)

            def v_load(h):
                for b in range(NS):
                    act.dma_start(vc2[:, b, :, :], mem_cache[1, h, :, b]).then_inc(vc_in, 16)
            def kv_tile(p, j, i, before):
                act.wait_ge(projected, p.c(j, i) + 1)
                act.wait_ge(*before)
                copy(kvr[:, j, :], bank[p.outs[j]][:, 0:NP]).then_inc(evac[p.outs[j]], 1)
                split_hi(act, p, j, i)

            for n in range(6):
                kv_tile(PH_KV, n % 3, n // 3, V_KV.at(f"t{n % 3}", n // 3 - 1))
                if n < 4:
                    normed_hi(0, PC_XPRE, n)
            act.wait_ge(*V_N[0].at("lo15"))
            v_load(0)
            with act.Fori(2, 5) as i:
                for j in range(3):
                    kv_tile(PH_KV, j, i, V_KV.at(f"t{j}", i - 1))
            kv_tile(PH_KV_E, 0, 0, V_KV.at("t0", 4))

            def x_piece(p, h):
                if p == 0:
                    act.wait_ge(*P_X.at(f"qs_{h}"))
                    copy(qtok[:, :], bank[4][0:NS, 0:NP]).then_inc(A_X(f"qt_{h}"), 1)
                    act.wait_ge(*V_X.at(f"mxs_{h}"))
                    if h:
                        act.wait_ge(*P_X.at(f"pt_{h - 1}"))
                    for m in range(2):
                        nc.scalar.activation(xp[:, m, :], bank[3][:, m * NP:(m + 1) * NP], ACT.Exp, scale=1.0 / 16,
                                             bias=xst[:, 2 + m:3 + m], accum_out=xst[:, 4 + m:5 + m])\
                            .then_inc(A_X(f"e{m}_{h}"), 1)
                if p == 1:
                    act.wait_ge(*P_X.at(f"pt_{h}"))
                    copy(xpT[:, :, :].rearrange("p m q -> p (m q)"), bank[3][:, :]).then_inc(A_X(f"pt_{h}"), 1)
                if p == 2:
                    act.wait_ge(*P_X.at(f"o_{h}"))
                    copy(o_hi[:, 2 * h:2 * h + 2, 0:NP], bank[4][:, :].rearrange("p (t q) -> p t q", q=NP))\
                        .then_inc(A_X(f"oh_{h}"), 1)
                if p == 3:
                    act.wait_ge(*V_X.at(f"smxs_{h}"))
                    if h:
                        act.wait_ge(*P_X.at(f"ps_{h - 1}"))
                    nc.scalar.activation(ssx[:, :], bank[7][0:NS, 0:NP], ACT.Exp, scale=1.0 / 16, bias=xss[:, 1:2],
                                         accum_out=xss[:, 2:3]).then_inc(A_X(f"se_{h}"), 1)
                if p == 4:
                    act.wait_ge(*P_X.at(f"ps_{h}"))
                    copy(xps[:, :, :].rearrange("p m b -> p (m b)"), bank[7][:, 256:272]).then_inc(A_X(f"ps_{h}"), 1)
                if p == 5:
                    act.wait_ge(*P_X.at(f"pv_{h}"))
                    copy(o_hi[:, 2 * h:2 * h + 2, NP:T], bank[7][:, 272:288].rearrange("p (t b) -> p t b", b=NS))\
                        .then_inc(A_X(f"ohs_{h}"), 1)
                    if h < 3:
                        v_load(h + 1)
            for s, pieces in enumerate(X_ORDER):
                if s < 8:
                    act.wait_ge(projected, PH_XQ.c(s) + 1)
                    if s == 0:
                        act.wait_ge(mem_out[0], 16)
                    if s >= 4:
                        act.wait_ge(*P_X.at(f"qs_{s // 2 - 2}"))
                    copy(qT[:, s % 4, :], bank[PH_XQ.outs[s]][:, 0:T]).then_inc(evac[PH_XQ.outs[s]], 1)
                    split_hi(act, PH_XQ, s)
                for p, h in pieces:
                    x_piece(p, h)

            def xo_tile(p, S, j, r, i):
                k = 2 * j + r
                if S == "xo":
                    before = V_OUT["xo"].at(f"acc{(k + 3) % 6}", i - (k < 3))
                else:
                    before = V_OUT["xo"].at(f"acc{k + 3}", 1) if k < 3 else V_OUT["xo_end"].at(f"acc{k - 3}")
                evacuate(p, j, k, i, (i * 6 if S == "xo" else 12) + k, before)
            with act.Fori(0, 2) as i:
                for j in range(3):
                    for r in range(2):
                        xo_tile(PH_XO, "xo", j, r, i)
                    split_hi(act, PH_XO, j, i)
            for j in range(2):
                for r in range(2):
                    xo_tile(PH_XO_E, "xo_end", j, r, 0)
                split_hi(act, PH_XO_E, j)
            norm(1, PC_FPRE)

            for half, (up, up_e, down, down_e) in enumerate(PH_FFN):
                def conv(p, S, V, j, i, n):
                    kind, q = j % 2, j // 2
                    col = half * FH + kind * FT
                    if kind:
                        act.wait_ge(*p.saved(j - 1, i))
                        g = cg[:, q, :]
                        nc.scalar.activation(g, g, ACT.Gelu_apprx_tanh).then_inc(S(f"g{q}"), 1)
                    act.wait_ge(projected, p.c(j, i) + 1)
                    if V is V_F[half]:
                        before = V.at(f"lo{q}", i - 1)
                    else:
                        before = V_F[half].at("lo0", 6)
                    act.wait_ge(*before)
                    c = (cg, cv)[kind][:, q, :]
                    nc.scalar.activation(c, bank[p.outs[j]][:, 0:T], ACT.Identity, scale=param(PC_CW + 176 + col, n),
                                         bias=param(PC_CB + col, n)).then_inc(S(f"c{j}"), 1)
                    copy(unew[:, ds(n + col, 1), :], bank[p.outs[j]][:, None, NP - 2:T]).then_inc(S(f"n{j}"), 1)
                    if kind:
                        act.wait_ge(*V.at(f"m{q}", i))
                        copy(y_hi[:, ds(n, 1), :], cv[:, q:q + 1, :]).then_inc(S(f"hi{q}"), 1)
                    split_hi(act, p, j, i)
                with act.Fori(0, 7) as i:
                    for j in range(6):
                        conv(up, A_F[half], V_F[half], j, i, i * 3 + j // 2)
                for j in range(2):
                    conv(up_e, A_FE[half], V_FE[half], j, 0, 21)

                def down_tile(p, S, k, i, n):
                    for r in range(2):
                        act.wait_ge(projected, p.c(2 * k + r, i) + 1)
                        if r and half == 0:
                            copy(merged[:, ds(n, 1), :], bank[p.outs[k]][:, None, 0:T]).then_inc(evac[p.outs[k]], 1)
                        if more(p, 2 * k + r, i):
                            split_hi(act, p, 2 * k + r, i)
                        if r and half == 1:
                            act.wait_ge(*p.saved(k, i))
                            act.wait_ge(*(V_OUT["down"].at(f"acc{k}", i - 1) if S == "down" else V_OUT["down"].at("acc0", 4)))
                            nc.scalar.activation(sqr[:, k:k + 1, :], merged[:, ds(n, 1), :], ACT.Square)\
                                .then_inc(A_OUT[S](f"sq{k}"), 1)
                with act.Fori(0, 4) as i:
                    for k in range(3):
                        down_tile(down, "down", k, i, i * 3 + k)
                for k in range(3):
                    down_tile(down, "down", k, 4, 12 + k)
                down_tile(down_e, "down_end", 0, 0, 15)
            norm(2, None)

            for c in range(4):
                act.wait_ge(*P_Y.at(f"y{c}"))
                copy(ytok[:, 0, c * 512:c * 512 + 512], bank[(3, 6)[c % 2]][:, :]).then_inc(A_Y(f"y{c}"), 1)
                copy(ytok_s[:, c * 512:c * 512 + 512], bank[(5, 0)[c % 2]][0:NS, :]).then_inc(A_Y(f"z{c}"), 1)

        @block.tensor
        def _(pe):
            pe.wait_ge(*G_SET.at("ident"))
            pe.wait_ge(par_loaded, 14 * 16)
            for g, (rows, c0) in enumerate([(P, 0), (104, P), (88, 232), (88, 320), (88, 408)]):
                mm = turn(bank[7][:, c0:c0 + rows], prow[0:rows, g, :], rows)
            mm.then_inc(P_SET("par"), 1)
            for t in range(KB):
                if t >= 4:
                    pe.wait_ge(*V_SET.at(f"lo{t - 4}"))
                if t == 0:
                    pe.wait_ge(*A_SET.at("sx2"))
                    pe.wait_ge(*V_SET.at("sx1"))
                out = bank[3 + t % 4]
                turn(out[:, 0:P], xtok[:, 0, t * P:t * P + P], P)
                turn(out[:, P:NP], xtok[:, 1, t * P:t * P + P], P)
                turn(out[:, NP:T], xtok_s[:, t * P:t * P + P], NS).then_inc(P_SET(f"x{t}"), 1)

            H_BLOCKS = over(h_hi, h_lo)
            product(pe, PH_GA, 0, 0, 0, H_BLOCKS, each=lambda n: V_SET.at(f"lo{n}")).then_inc(projected, 1)
            pe.wait_ge(*V_SET.at("lo15"))
            pe.wait_ge(bias_loaded, 32)
            pe.wait_ge(*G_SET.at("neg"))
            for g in range(3):
                nc.tensor.matmul(bank[3 + g][0:8, 0:383], relx[:, 8 * g:8 * g + 8], onehot[:, 383 * g:383 * g + 383],
                                 start=True, stop=True).then_inc(P_SET(f"tz{g}"), 1)
            off = 3 * 383
            at0 = 0
            for g in range(3):
                nc.tensor.matmul(bank[6][0:8, at0:at0 + DSLOTS[g]], relx[:, 8 * g:8 * g + 8],
                                 onehot[:, off + at0:off + at0 + DSLOTS[g]], start=True, stop=True)
                at0 += DSLOTS[g]
            for g in range(3):
                mm = nc.tensor.matmul(bank[6][0:8, SSEEN + g:SSEEN + g + 1], relx[:, 8 * g:8 * g + 8],
                                      onehot[:, off + SSEEN + g:off + SSEEN + g + 1], start=True, stop=True)
            mm.then_inc(P_SET("sb"), 1)

            def gla_head(h, tail):
                p = PH_GLA
                for j in range(12):
                    product(pe, p, j, j, h, H_BLOCKS).then_inc(projected, 1)
                    tail(j)
                    if j == 4:
                        pe.wait_ge(*V_GLA.at("kh1", h))
                        for m in range(2):
                            for t in range(2):
                                mm = turn(bank[3][:, m * NP + t * P:m * NP + t * P + P], g_kh[:, t, m * P:m * P + P], P)
                        mm.then_inc(P_GLA("t_kh"), 1)
                    if j == 5:
                        pe.wait_ge(*p.saved(3, h))
                        pe.wait_ge(*A_GLA.at("o0", h - 1))
                        for m in range(2):
                            for t in range(2):
                                mm = nc.tensor.matmul(bank[4][:, m * P:m * P + P], g_kt[:, t, m * P:m * P + P],
                                                      g_qt[:, t, m * P:m * P + P], start=t == 0, stop=t == 1)
                        mm.then_inc(P_GLA("a"), 1)
                    if j == 8:
                        pe.wait_ge(*p.saved(7, h))
                        pe.wait_ge(*V_GLA.at("S3_1", h - 1))
                        for m in range(2):
                            for v in range(4):
                                mm = turn(bank[6 + m][:, v * P:v * P + P], g_vT[:, v, m * P:m * P + P], P)
                            mm.then_inc(P_GLA(f"t_v{m}"), 1)
                        pe.wait_ge(*V_GT.at("var", h - 1))
                        for v in range(4):
                            mm = turn(bank[5][0:NS, v * P:v * P + P], g_vT[:, v, NP:T], P)
                        mm.then_inc(P_GLA("t_vs"), 1)

                    def intra(m, name):
                        for v in range(4):
                            mm = nc.tensor.matmul(bank[4 + m][:, v * P:v * P + P], g_vtok[:, m, v * P:v * P + P],
                                                  g_at[:, m, :], start=v == 0, stop=False, skip_group_check=True)
                        mm.then_inc(P_GLA(name), 1)

                    def inter(n, name):
                        for v in range(4):
                            for t in range(2):
                                c = v * P + 64 * (n % 2)
                                mm = nc.tensor.matmul(bank[4 + n // 2][:, c:c + 64], g_S[:, t, v * P:v * P + P],
                                                      g_qt[:, t, 64 * n:64 * n + 64], start=False,
                                                      stop=v == 3 and t == 1, skip_group_check=True)
                        mm.then_inc(P_GLA(name), 1)

                    def update(n, name):
                        q, m = 64 * (n % 2), n // 2
                        for t in range(2):
                            mm = nc.tensor.matmul(bank[6 + t][:, :], g_khtok[q:q + 64, m, t * P:t * P + P],
                                                  g_vtok[q:q + 64, m, :], start=True, stop=True)
                        mm.then_inc(P_GLA(name), 1)

                    if j == 9:
                        pe.wait_ge(*V_GLA.at("vtok1", h))
                        pe.wait_ge(*G_GLA.at("mask", h))
                        intra(0, "o0a")
                        update(0, "u0")
                    if j == 10:
                        pe.wait_ge(*A_GLA.at("vs", h))
                        intra(1, "o1a")
                        pe.wait_ge(*V_GLA.at("S0_1", h))
                        inter(1, "i1")
                        update(1, "u1")
                    if j == 11:
                        for n in (2, 3):
                            pe.wait_ge(*V_GLA.at(f"S{n - 1}_1", h))
                            inter(n, f"i{n}")
                            update(n, f"u{n}")

            def gla_tail(k, h):
                if 1 <= k < 6:
                    for b in TAIL_SEQS[k - 1]:
                        pe.wait_ge(*V_GT.at(f"sn{b}_1", h))
                        if b == 0:
                            pe.wait_ge(*A_GLA.at("o1", h))
                        for t in range(2):
                            mm = nc.tensor.matmul(bank[5][0:NS, :], g_qm[:, t, b, :], g_Ss[b % 4][:, t, :],
                                                  start=b + t == 0, stop=b + t == NS)
                        mm.then_inc(P_GT(f"os{b}"), 1)
                if k == 6:
                    pe.wait_ge(*A_GT.at("om", h))
                    for v in range(4):
                        mm = nc.tensor.matmul(bank[5][:, v * NS:(v + 1) * NS], g_om[:, v * P:v * P + P],
                                              ident[0:NS, 0:NS], start=True, stop=True)
                    mm.then_inc(P_GT("ot"), 1)
                if k == 7:
                    pe.wait_ge(*A_GT.at("sq", h))
                    for v in range(4):
                        mm = nc.tensor.matmul(bank[5][:, 32:32 + T], ones[:, :], g_sq[:, v, :], start=v == 0, stop=v == 3)
                    mm.then_inc(P_GT("ssq"), 1)

            pe.wait_ge(*PH_GA.saved(0))
            pe.wait_ge(a2_loaded, 16)
            for t in range(8):
                if t == 0:
                    pe.wait_ge(*V_SET.at("sb"))
                if t >= 4:
                    pe.wait_ge(*V_PRE.at(f"z{t - 4}"))
                nc.tensor.matmul(bank[3 + t % 4][:, 0:T], w_a2[:, t * P:t * P + P], ga[:, :], start=True, stop=True)\
                    .then_inc(P_PRE(f"z{t}"), 1)
            gla_head(0, lambda k: None)
            with pe.Fori(1, 4) as h:
                gla_head(h, lambda k: gla_tail(k, h - 1))

            YG_BLOCKS = over(y_hi, y_lo)
            for j in range(3):
                product(pe, PH_GLA_G, j, j, 0, H_BLOCKS).then_inc(projected, 1)
                gla_tail(j, 3)
            for k in range(3, 9):
                gla_tail(k, 3)

            def y_ready(n):
                return V_GT.at("yl3", 2) if n < 12 else V_GT.at(f"yl{n - 12}", 3)
            with pe.Fori(0, 4) as i:
                for j in range(6):
                    product(pe, PH_GLA_B, j, j, i, H_BLOCKS if j % 2 else YG_BLOCKS, each=None if j else y_ready)\
                        .then_inc(projected, 1)
            for j in range(5):
                product(pe, PH_GLA_E, j, j, 0, H_BLOCKS if j == 1 else YG_BLOCKS).then_inc(projected, 1)

            def dil_scores(h, g):
                p = PH_DIL
                pe.wait_ge(*p.saved(3 * g + 1, h))
                if g == 0:
                    pe.wait_ge(*A_DT.at("pt2", h - 1))
                    pe.wait_ge(*V_DT.at("pt1", h - 1))
                else:
                    pe.wait_ge(*V_DIL.at(f"b0_{g - 1}", h))
                q, k = qkvT[:, 3 * g, :], qkvT[:, 3 * g + 1, :]
                late = (bank[3][:, 0:NP], bank[3][:, NP:2 * NP], bank[4][:, 0:NP])[g]
                nc.tensor.matmul(late, q[:, P:NP], k[:, 0:NP], start=True, stop=True)
                nc.tensor.matmul(bank[5][:, g * P:g * P + P], q[:, 0:P], k[:, 0:P], start=True, stop=True)\
                    .then_inc(P_DIL(f"s_{g}"), 1)

            def dil_turn(h, g, st):
                pe.wait_ge(*PH_DIL.saved(3 * g + 2, h))
                pe.wait_ge(*(A_DT.at("kv2", h - 1) if g == 0 else A_DIL.at(f"kv{g - 1}", h)))
                for v in range(2):
                    for m in range(2):
                        mm = turn(bank[6][:, (2 * v + m) * P:(2 * v + m + 1) * P],
                                  qkvT[:, 3 * g + 1 + v, m * P:m * P + P], P)
                mm.then_inc(st(f"kv{g}"), 1)
                pe.wait_ge(*(V_DT.at("yl", h - 1) if g == 0 else V_DT.at("yls", h - 1) if g == 1 else V_DIL.at("qk1", h)))
                for v in range(3):
                    mm = turn(bank[7][0:NS, v * P:v * P + P], qkvT[:, 3 * g + v, NP:T], P)
                mm.then_inc(st(f"qs{g}"), 1)

            def dil_body(h, tail):
                for j in range(9):
                    product(pe, PH_DIL, j, j, h, H_BLOCKS).then_inc(projected, 1)
                    if j == 5:
                        pe.wait_ge(*V_DIL.at("qk0", h))
                    tail(j)
                    if j % 3 == 2:
                        dil_scores(h, j // 3)
                    if j in (3, 8):
                        dil_turn(h, (3, 8).index(j), P_DIL)

            def dil_tail(k, h):
                if k == 0:
                    dil_turn(h, 2, P_DT)
                if k == 1:
                    pe.wait_ge(*V_DIL.at("n0", h))
                    for g in range(3):
                        for n, src in enumerate((s0[:, g, :], s1[:, g, 0:P], s1[:, g, P:NP])):
                            mm = turn(bank[3 + g][:, n * P:n * P + P], src, P)
                        mm.then_inc(P_DT(f"pt{g}"), 1)
                if k == 2:
                    pe.wait_ge(*A_DT.at("kv2", h))
                    pe.wait_ge(*V_DT.at("qk2", h))
                    pe.wait_ge(*A_DT.at("pt2", h))
                    pe.wait_ge(*V_DT.at("pt1", h))
                    for g in range(3):
                        nc.tensor.matmul(bank[7][:, 0:NP], kvtok[:, g, 1, 0, :], pT[:, g, 0:NP], start=g == 0, stop=False,
                                         skip_group_check=True)
                        mm = nc.tensor.matmul(bank[7][:, P:NP], kvtok[:, g, 1, 1, :], pT[:, g, NP:384], start=False,
                                              stop=g == 2, skip_group_check=True)
                    mm.then_inc(P_DT("pv"), 1)
                if k == 5:
                    pe.wait_ge(*V_DT.at("sc2", h))
                    for g in range(3):
                        n = DSLOTS[g]
                        mm = turn(bank[7][0:NS, g * P:g * P + n], sct[0:n, g, :], n)
                    mm.then_inc(P_DT("sct"), 1)
                if k == 6:
                    pe.wait_ge(*V_DT.at("sn", h))
                    for g in range(3):
                        n = DSLOTS[g]
                        mm = nc.tensor.matmul(bank[7][0:n, NS * g:NS * g + NS], ssamp[:, g * P:g * P + n],
                                              ident[0:NS, 0:NS], start=True, stop=True)
                    mm.then_inc(P_DT("pst"), 1)
                if k == 7:
                    pe.wait_ge(*A_DT.at("ps1", h))
                    pe.wait_ge(*V_DT.at("dg2", h))
                    pe.wait_ge(v_in, h * 48 + 48)
                    for g in range(3):
                        nc.tensor.matmul(bank[7][:, 32:40], vnew[:, g, :], pdiag[:, g, :], start=g == 0, stop=False,
                                         skip_group_check=True)
                    for g in range(3):
                        n = DSLOTS[g]
                        for b in range(NS):
                            mm = nc.tensor.matmul(bank[7][:, 32 + b:33 + b], vcache[0:n, g, b, :], psT[0:n, g, b:b + 1],
                                                  start=False, stop=g == 2 and b == NS - 1, skip_group_check=True)
                    mm.then_inc(P_DT("pvs"), 1)

            dil_body(0, lambda k: None)
            with pe.Fori(1, 8) as h:
                dil_body(h, lambda k: dil_tail(k, h - 1))

            def pair_products(p_g, p_b, p_e, x_hi, x_lo, tail, ready):
                for j in range(4):
                    product(pe, p_g, j, j, 0, H_BLOCKS).then_inc(projected, 1)
                    tail(j)
                for k in range(4, 8):
                    tail(k)
                for s, v in ready:
                    pe.wait_ge(s, v)

                def pair(p, j, k, i):
                    for r in range(2):
                        mm = product(pe, p, j, k + r, i, over(x_hi, x_lo, 8, r * P, 0, 2 * P), fresh=r == 0)
                    mm.then_inc(projected, 1)
                with pe.Fori(0, 3) as i:
                    for q in range(2):
                        pair(p_b, 3 * q, 4 * q, i)
                        for r in range(2):
                            product(pe, p_b, 3 * q + 1 + r, 4 * q + 2 + r, i, H_BLOCKS).then_inc(projected, 1)
                for q in range(2):
                    pair(p_e, q, 2 * q, 0)
            pair_products(PH_DIL_G, PH_DIL_B, PH_DIL_E, y_hi, y_lo, lambda k: dil_tail(k, 7), [V_DT.at("yls", 7)])

            def new_rows(g):
                pe.wait_ge(*A_PO.at(f"h{g}"))
                if g >= 2:
                    pe.wait_ge(*V_PO.at(f"ub{g - 2}"))
                out = bank[4 + 2 * (g % 2)]
                for t in range(2):
                    u = u_ctx[:, 2 * (g % 2) + t, :]
                    turn(out[0:15, t * P:t * P + P], u[:, UP + NP - 15:UP + NP], P)
                    mm = turn(out[0:NS, NP + t * P:NP + t * P + P], u[:, US + 15:US + 16 * NS:16], P)
                mm.then_inc(P_PO(f"o{g}"), 1)
            pe.wait_ge(ph_in, 16)
            for j in range(8):
                g = j // 2
                product(pe, PH_PU, j, j, 0, H_BLOCKS).then_inc(projected, 1)
                if j % 2 == 0:
                    if g >= 2:
                        pe.wait_ge(*A_PO.at(f"h{g - 2}"))
                    for t in range(2):
                        mm = turn(bank[3 + 2 * (g % 2)][:, t * 120:t * 120 + 120],
                                  ptok[:, (2 * g + t) * P:(2 * g + t + 1) * P], 120)
                    mm.then_inc(P_PO(f"h{g}"), 1)
                    if g:
                        new_rows(g - 1)

            def pool_products(k):
                if k != 4:
                    return
                for t in range(8):
                    g, n = t // 2, t % 2
                    if n == 0:
                        pe.wait_ge(*V_PO.at(f"l{g}"))
                    mm = product(pe, PH_PW, 0, t, 0, [((2 * g + k) * 2 * P + n * P, y_hi[:, 8 + 2 * g + k, :],
                                                       y_lo[:, 8 + 2 * g + k, :]) for k in range(2)], fresh=t == 0)
                    mm.then_inc(P_PO(f"w{t}") if t < 7 else projected, 1)
                new_rows(3)
            pair_products(PH_PL_G, PH_PL_B, PH_PL_E, y_hi, y_lo, pool_products, [PH_PW.saved(7)])

            MERGED_BLOCKS = over(h_hi, h_lo)
            with pe.Fori(0, 3) as i:
                for j in range(3):
                    product(pe, PH_MO, j, j, i, MERGED_BLOCKS, each=(lambda n: V_MH.at(f"m{n // 4}")) if j == 0 else None)\
                        .then_inc(projected, 1)
            for t in range(KB):
                pe.wait_ge(*(V_MM.at(f"lo{t - 4}") if t >= 4 else A_MM.at("x1")))
                for m in range(2):
                    mm = turn(bank[3 + t % 4][:, m * P:m * P + P], memtok[:, m, t * P:t * P + P], P)
                mm.then_inc(P_MM(f"x{t}"), 1)
            with pe.Fori(3, 5) as i:
                for j in range(3):
                    product(pe, PH_MO, j, j, i, MERGED_BLOCKS).then_inc(projected, 1)
            product(pe, PH_MO_E, 0, 0, 0, MERGED_BLOCKS).then_inc(projected, 1)

            def norm(n, last_acc):
                pe.wait_ge(*last_acc)
                nc.tensor.matmul(bank[7][:, 0:T], ones[:, :], acc[:, :], start=True, stop=True).then_inc(P_N[n]("sum"), 1)
                if n == 0:
                    product(pe, PH_KV, 0, 0, 0, over(hm_hi, hm_lo), cols=NP).then_inc(projected, 1)
                    pe.wait_ge(x2_in, 64)
                    for t in range(KB):
                        pe.wait_ge(*(V_N[0].at(f"x{t - 3}") if t >= 3 else V_MM.at("lo15")))
                        out = bank[3 + t % 3]
                        for m in range(2):
                            turn(out[:, m * P:m * P + P], xtok2[:, m, t * P:t * P + P], P)
                        turn(out[:, NP:T], xtok2_s[t // 8][:, (t % 8) * P:(t % 8 + 1) * P], NS).then_inc(P_N[n](f"xt{t}"), 1)

            def norm_sums(n):
                for t in range(KB):
                    pe.wait_ge(*A_N[n].at(f"q{t}"))
                    nc.tensor.matmul(bank[7][:, 0:T], ones[:, :], sqr[:, t % 3, :], start=t == 0, stop=t == KB - 1)\
                        .then_inc(P_N[n](f"s{t}"), 1)
            norm(0, V_OUT["mix_end"].at("acc0"))
            norm_sums(0)

            MEM_BLOCKS = over(hm_hi, hm_lo)

            def kv_tile(p, Pt, j, i):
                product(pe, p, j, j, i, MEM_BLOCKS, cols=NP).then_inc(projected, 1)

            def kv_turn(p, Pt, j, i, before):
                pe.wait_ge(*p.saved(j, i))
                pe.wait_ge(*before)
                for m in range(2):
                    mm = turn(bank[6][:, m * P:m * P + P], kvr[:, j, m * P:m * P + P], P)
                mm.then_inc(Pt(f"t{j}"), 1)
            def kv_body(i):
                if isinstance(i, int):
                    for j in (1, 2):
                        kv_tile(PH_KV, P_KV, j, i)
                for j in range(3):
                    if not isinstance(i, int):
                        kv_tile(PH_KV, P_KV, j, i)
                    if j:
                        kv_turn(PH_KV, P_KV, j - 1, i, V_KV.at(f"t{(j + 1) % 3}", i if j == 2 else i - 1))
                    elif not isinstance(i, int):
                        kv_turn(PH_KV, P_KV, 2, i - 1, V_KV.at("t1", i - 1))
            kv_body(0)
            with pe.Fori(1, 5) as i:
                kv_body(i)
            kv_tile(PH_KV_E, P_KE, 0, 0)
            kv_turn(PH_KV, P_KV, 2, 4, V_KV.at("t1", 4))
            kv_turn(PH_KV_E, P_KE, 0, 0, V_KV.at("t2", 4))

            def spread(h, n):
                for b in (2 * n, 2 * n + 1):
                    mm = nc.tensor.matmul(bank[5 + n % 2][:, (b % 2) * NP:(b % 2 + 1) * NP],
                                          ident[0:NS, b:b + 1].to_broadcast([NS, P]), qtok[:, :], start=True, stop=True)
                mm.then_inc(P_X(f"sp{n}_{h}"), 1)

            def x_piece(p, h):
                if p == 0:
                    for t in range(2):
                        pe.wait_ge(*PH_XQ.saved(2 * h + t))
                    if h:
                        pe.wait_ge(*A_X.at(f"pt_{h - 1}"))
                    for m in range(2):
                        for t in range(2):
                            mm = nc.tensor.matmul(bank[3][:, m * NP:(m + 1) * NP], qT[:, (2 * h + t) % 4, m * P:m * P + P],
                                                  kT[h // 2][:, (2 * h + t) % 4, :], start=t == 0, stop=t == 1)
                    mm.then_inc(P_X(f"sc_{h}"), 1)
                    if h:
                        pe.wait_ge(*A_X.at(f"oh_{h - 1}"))
                        pe.wait_ge(*V_X.at(f"ol_{h - 1}"))
                    for t in range(2):
                        mm = turn(bank[4][0:NS, t * P:t * P + P], qT[:, (2 * h + t) % 4, NP:T], P)
                    mm.then_inc(P_X(f"qs_{h}"), 1)
                if p == 1:
                    pe.wait_ge(*V_X.at(f"n1_{h}"))
                    for mt in range(2):
                        for m in range(2):
                            mm = turn(bank[3][:, mt * NP + m * P:mt * NP + m * P + P], xp[:, m, mt * P:mt * P + P], P)
                    mm.then_inc(P_X(f"pt_{h}"), 1)
                    pe.wait_ge(*A_X.at(f"qt_{h}"))
                    pe.wait_ge(*(V_X.at(f"k7_{h - 1}") if h else V_KE.at("t0")))
                    spread(h, 0)
                    spread(h, 1)
                if p == 2:
                    pe.wait_ge(*A_X.at(f"pt_{h}"))
                    for t in range(2):
                        for mt in range(2):
                            e0 = h * NP + t * P
                            mm = nc.tensor.matmul(bank[4][:, t * NP:(t + 1) * NP], kvtok2[:, 1, mt, e0:e0 + P],
                                                  xpT[:, mt, :], start=mt == 0, stop=mt == 1)
                    mm.then_inc(P_X(f"o_{h}"), 1)
                    for n in (2, 3):
                        pe.wait_ge(*V_X.at(f"k{2 * (n - 2) + 1}_{h}"))
                        spread(h, n)
                if p == 3:
                    pe.wait_ge(*V_X.at(f"k7_{h}"))
                    if h:
                        pe.wait_ge(*V_X.at(f"ols_{h - 1}"))
                    for mt in range(2):
                        mm = turn(bank[7][0:NS, mt * P:mt * P + P], xsct[:, mt, :], P)
                    mm.then_inc(P_X(f"sct_{h}"), 1)
                if p == 4:
                    pe.wait_ge(*V_X.at(f"sn_{h}"))
                    for mt in range(2):
                        mm = nc.tensor.matmul(bank[7][:, 256 + mt * NS:264 + mt * NS], ssx[:, mt * P:mt * P + P],
                                              ident[0:NS, 0:NS], start=True, stop=True)
                    mm.then_inc(P_X(f"ps_{h}"), 1)
                if p == 5:
                    pe.wait_ge(*A_X.at(f"ps_{h}"))
                    pe.wait_ge(vc_in, (h + 1) * NS * 16)
                    for b in range(NS):
                        for t in range(2):
                            c = 272 + t * NS + b
                            for mt in range(2):
                                mm = nc.tensor.matmul(bank[7][:, c:c + 1], vc2[:, b, mt, t * P:t * P + P],
                                                      xps[:, mt, b:b + 1], start=mt == 0, stop=mt == 1)
                    mm.then_inc(P_X(f"pv_{h}"), 1)
            pe.wait_ge(*V_N[0].at("lo15"))
            for s, pieces in enumerate(X_ORDER):
                if s < 8:
                    product(pe, PH_XQ, s, s, 0, H_BLOCKS).then_inc(projected, 1)
                for p, h in pieces:
                    x_piece(p, h)

            pe.wait_ge(*V_X.at("ols_3"))

            def xo_slot(p, j, i):
                for r in range(2):
                    mm = product(pe, p, j, 2 * j + r, i, over(o_hi, o_lo, 8, r * P, 0, 2 * P), fresh=r == 0)
                mm.then_inc(projected, 1)
            with pe.Fori(0, 2) as i:
                for j in range(3):
                    xo_slot(PH_XO, j, i)
            for j in range(2):
                xo_slot(PH_XO_E, j, 0)
            norm(1, V_OUT["xo_end"].at("acc3"))
            pe.wait_ge(hr_in, 16)
            for c in range(4):
                for r in range(4):
                    mm = turn(bank[3 + c][:, r * 2 * FT:(r + 1) * 2 * FT], hrows[:, 4 * c + r, :], 2 * FT)
                mm.then_inc(P_H(f"h{c}"), 1)
            norm_sums(1)
            for half, (up, up_e, down, down_e) in enumerate(PH_FFN):
                with pe.Fori(0, 7) as i:
                    for j in range(6):
                        product(pe, up, j, j, i, H_BLOCKS, each=(lambda n: V_N[1].at(f"lo{n}")) if j + half == 0 else None)\
                            .then_inc(projected, 1)
                for j in range(2):
                    product(pe, up_e, j, j, 0, H_BLOCKS).then_inc(projected, 1)

                def down_slot(p, k, r, i):
                    product(pe, p, 2 * k + r, k, i, over(y_hi, y_lo, FH // 2, 0, r * FH // 2), first=r == 0,
                            last=r == 1).then_inc(projected, 1)
                pe.wait_ge(*V_F[half].at("lo2", 6))
                for k in range(3):
                    for r in range(2):
                        if k == 0 and r == 1:
                            pe.wait_ge(*V_FE[half].at("lo0"))
                        down_slot(down, k, r, 0)
                with pe.Fori(1, 5) as i:
                    for k in range(3):
                        for r in range(2):
                            down_slot(down, k, r, i)
                if half == 1:
                    for c in range(5):
                        for r in range(2):
                            mm = turn(bank[3 + c][0:2 * FT, r * P:r * P + P], unew[:, :, 2 * c + r], P)
                        mm.then_inc(P_Y(f"c{c}"), 1)
                for r in range(2):
                    down_slot(down_e, 0, r, 0)
            norm(2, V_OUT["down_end"].at("acc0"))
            for c in range(4):
                pe.wait_ge(*V_N[2].at(f"x{4 * c + 3}"))
                a, b, z = ((3, 4, 5), (6, 7, 0))[c % 2]
                if c >= 2:
                    pe.wait_ge(*A_Y.at(f"z{c - 2}"))
                    pe.wait_ge(*V_Y.at(f"y{c - 2}"))
                else:
                    pe.wait_ge(*V_Y.at("c4"))
                    pe.wait_ge(*V_N[2].at("var"))
                for t in range(4):
                    for m in range(2):
                        turn(bank[(a, b)[m]][:, t * P:t * P + P], xres[:, 4 * c + t, m * P:m * P + P], P)
                    mm = turn(bank[z][0:NS, t * P:t * P + P], xres[:, 4 * c + t, NP:T], P)
                mm.then_inc(P_Y(f"y{c}"), 1)

        @block.vector
        def _(dve):
            dve.wait_ge(x_loaded, 48)
            dve.wait_ge(*G_SET.at("stat"))
            nc.vector.tensor_tensor_reduce(out=junk[1][:, :], in0=xtok[:, 1, :], in1=xtok[:, 1, :], scale=1.0, scalar=0.0,
                                           op0=ALU.mult, op1=ALU.add, accum_out=stat[:, 1:2]).then_inc(V_SET("sq1"), 1)
            dve.wait_ge(*V_SET.at("sq1"))
            dve.wait_ge(*A_SET.at("sq2"))
            nc.vector.tensor_scalar(stat[:, 3:6], stat[:, 0:3], 1.0 / D, EPS, ALU.mult, ALU.add).then_inc(V_SET("var"), 1)
            dve.wait_ge(*A_SET.at("root"))
            nc.vector.reciprocal(stat[:, 9:12], stat[:, 6:9]).then_inc(V_SET("rstd"), 1)
            dve.wait_ge(*V_SET.at("rstd"))
            nc.vector.tensor_scalar(xtok[:, 1, :], xtok[:, 1, :], stat[:, 10:11], None, ALU.mult).then_inc(V_SET("sx1"), 1)
            dve.wait_ge(*P_SET.at("par"))
            nc.vector.tensor_copy(par[:, 0:PC_END], bank[7][:, 0:PC_END]).then_inc(V_SET("par"), 1)

            def first_lo(c):
                dve.wait_ge(hi_ready, c + 1)
                nc.vector.tensor_tensor(w_lo[:, c, :], raw[:, c, :], w_hi[:, c, :].bitcast(F32),
                                        ALU.subtract).then_inc(lo_ready, 1)
            for t in range(KB):
                dve.wait_ge(*A_SET.at(f"hi{t}"))
                nc.vector.scalar_tensor_tensor(out=h_lo[:, t, :], in0=bank[3 + t % 4][:, 0:T],
                                               scalar=param(PC_MIXPRE, t), in1=h_hi[:, t, :].bitcast(F32),
                                               op0=ALU.mult, op1=ALU.subtract).then_inc(V_SET(f"lo{t}"), 1)
                if t in (0, 9):
                    first_lo(t // 9)
            first_lo(2)
            for g in range(3):
                dve.wait_ge(*P_SET.at(f"tz{g}"))
                nc.vector.tensor_copy(toep[:, g, 0:383], bank[3 + g][0:8, 0:383]).then_inc(V_SET(f"tz{g}"), 1)
            dve.wait_ge(*P_SET.at("sb"))
            nc.vector.tensor_copy(sbias_all[:, 0:SSEEN + 3], bank[6][0:8, 0:SSEEN + 3]).then_inc(V_SET("sb"), 1)
            split_lo(dve, PH_GA, 0)
            for t in range(8):
                dve.wait_ge(*P_PRE.at(f"z{t}"))
                nc.vector.tensor_scalar(la[:, t, :], bank[3 + t % 4][:, 0:T], param(PC_BA, t), None, ALU.add)\
                    .then_inc(V_PRE(f"z{t}"), 1)
            dve.wait_ge(*A_PRE.at("ln"))
            nc.vector.scalar_tensor_tensor(out=la[:, :, :], in0=la[:, :, :], scalar=0.0, in1=gtmp[:, :, :],
                                           op0=ALU.min, op1=ALU.subtract).then_inc(V_PRE("min"), 1)
            dve.wait_ge(*V_PRE.at("min"))
            nc.vector.tensor_scalar(la[:, :, :], la[:, :, :], 1.0 / 16, None, ALU.mult).then_inc(V_PRE("scale"), 1)
            dve.wait_ge(*V_PRE.at("scale"))
            dve.wait_ge(*G_SET.at("keep"))
            for t in range(8):
                nc.vector.tensor_tensor_scan(la[:, t, 0:NP], scan_keep[:, :], la[:, t, 0:NP], 0.0,
                                             ALU.mult, ALU.add).then_inc(V_PRE(f"scan{t}"), 1)

            def gla_head(h, tail):
                p = PH_GLA
                for j in range(12):
                    ps = bank[p.outs[j]]
                    dve.wait_ge(projected, p.c(j, h) + 1)
                    if j == 0:
                        dve.wait_ge(*A_GLA.at("dec", h))
                    if j < 2:
                        nc.vector.tensor_scalar(g_qs[:, ds(h * 2 + j, 1), :], ps[:, None, NP:T], 1.0 / 16, None,
                                                ALU.mult).then_inc(V_GLA(f"qs{j}"), 1)
                        nc.vector.scalar_tensor_tensor(out=g_qt[:, j, :], in0=ps[:, 0:NP], scalar=1.0 / 16,
                                                       in1=g_qt[:, j, :], op0=ALU.mult, op1=ALU.mult)\
                            .then_inc(evac[p.outs[j]], 1)
                    elif j < 4:
                        t = j - 2
                        nc.vector.tensor_tensor(g_kh[:, t, :], ps[:, 0:NP], g_kh[:, t, :], ALU.mult)\
                            .then_inc(V_GLA(f"kh{t}"), 1)
                        nc.vector.tensor_copy(g_ks[:, ds(h * 2 + t, 1), :], ps[:, None, NP:T]).then_inc(V_GLA(f"ks{t}"), 1)
                        nc.vector.tensor_tensor(g_kt[:, t, :], ps[:, 0:NP], g_kt[:, t, :], ALU.mult)\
                            .then_inc(evac[p.outs[j]], 1)
                    split_lo(dve, p, j, h)
                    if j == 8:
                        for m in range(2):
                            dve.wait_ge(*P_GLA.at(f"t_v{m}", h))
                            nc.vector.tensor_copy(g_vtok[:, m, :], bank[6 + m][:, :]).then_inc(V_GLA(f"vtok{m}"), 1)
                    tail(j)
                    if j == 4:
                        dve.wait_ge(*P_GLA.at("t_kh", h))
                        nc.vector.tensor_copy(g_khtok[:, :, :].rearrange("p a b -> p (a b)"), bank[3][:, :])\
                            .then_inc(V_GLA("khtok"), 1)
                    if j >= 9:
                        for n in ([0], [1], [2, 3])[j - 9]:
                            dve.wait_ge(*P_GLA.at(f"u{n}", h))
                            if n == 0:
                                if not isinstance(h, int):
                                    dve.wait_ge(S_stored, h * 16)
                            else:
                                dve.wait_ge(*V_GLA.at(f"S{n - 1}_1", h))
                            for t in range(2):
                                if n == 0:
                                    nc.vector.tensor_copy(g_S[:, t, :], bank[6 + t][:, :]).then_inc(V_GLA(f"S0_{t}"), 1)
                                else:
                                    nc.vector.scalar_tensor_tensor(
                                        out=g_S[:, t, :], in0=g_S[:, t, :], scalar=g_dec[:, t, n:n + 1],
                                        in1=bank[6 + t][:, :], op0=ALU.mult, op1=ALU.add).then_inc(V_GLA(f"S{n}_{t}"), 1)

            def gla_tail(k, h):
                if k == 0:
                    dve.wait_ge(*P_GT.at("os7", h - 1))
                    dve.wait_ge(*V_GLA.at("qs1", h))
                    nc.vector.tensor_copy(g_qm[:, :, :, :].rearrange("p t b c -> p t (b c)")[:, :, 0:NS * NS:NS + 1],
                                          g_qs[:, ds(h * 2, 2), :]).then_inc(V_GT("qm"), 1)
                if k < 5:
                    for b in TAIL_SEQS[k]:
                        dve.wait_ge(vb_in[b // 2 % 2], h * 32 + (b // 4 * 16 + 16))
                        dve.wait_ge(*A_GT.at(f"sd{b}_1", h))
                        for t in range(2):
                            st = g_Ss[b % 4][:, t, :]
                            nc.vector.scalar_tensor_tensor(out=st, in0=g_vb[:, b % 4, :],
                                                           scalar=g_ks[:, ds(h * 2 + t, 1), b], in1=st,
                                                           op0=ALU.mult, op1=ALU.add).then_inc(V_GT(f"sn{b}_{t}"), 1)
                if k == 7:
                    dve.wait_ge(*P_GT.at("ssq", h))
                    nc.vector.tensor_scalar(g_var[:, :], bank[5][:, 32:32 + T], 1.0 / 512, EPS, ALU.mult, ALU.add)\
                        .then_inc(V_GT("var"), 1)
                    dve.wait_ge(*A_GT.at("root", h))
                    nc.vector.reciprocal(g_rstd[:, :], g_var[:, :]).then_inc(V_GT("rstd"), 1)
                    dve.wait_ge(*V_GT.at("rstd", h))
                    nc.vector.tensor_tensor(g_o[:, :, :], g_o[:, :, :], g_rstd[:, None, :].to_broadcast([P, 4, T]),
                                            ALU.mult).then_inc(V_GT("on"), 1)
                    dve.wait_ge(*V_GT.at("on", h))
                    nc.vector.tensor_tensor(g_o[:, :, :], g_o[:, :, :], g_sr[:, :, :], ALU.mult).then_inc(V_GT("osr"), 1)
                if k == 8:
                    dve.wait_ge(*V_GT.at("osr", h))
                    for v in range(4):
                        dve.wait_ge(*A_GT.at(f"yh{v}", h))
                        row = ds(h * 4 + v, 1)
                        nc.vector.scalar_tensor_tensor(out=y_lo[:, row, :], in0=g_o[:, v:v + 1, :],
                                                       scalar=param(PC_GNORM, h * 4 + v),
                                                       in1=y_hi[:, row, :].bitcast(F32),
                                                       op0=ALU.mult, op1=ALU.subtract).then_inc(V_GT(f"yl{v}"), 1)

            gla_head(0, lambda k: None)
            with dve.Fori(1, 4) as h:
                gla_head(h, lambda k: gla_tail(k, h - 1))
            for j in range(3):
                dve.wait_ge(projected, PH_GLA_G.c(j) + 1)
                split_lo(dve, PH_GLA_G, j)
                gla_tail(j, 3)
            for k in range(3, 9):
                gla_tail(k, 3)

            def gated(p, j, k, i, g, n, gate_saved):
                dve.wait_ge(projected, p.c(j, i) + 1)
                dve.wait_ge(*gate_saved)
                nc.vector.tensor_tensor(merged[:, ds(n, 1), :], gates[:, g:g + 1, :], bank[p.outs[k]][:, None, 0:T],
                                        ALU.mult).then_inc(evac[p.outs[k]], 1)
            dve.wait_ge(ss_out[1], 4 * 64)
            with dve.Fori(0, 4) as i:
                p = PH_GLA_B
                for j in range(6):
                    if j % 2 == 0:
                        n = j // 2
                        b = p.outs[j + 1]
                        before = p.freed(j + 1, i)
                        gated(p, j, j, i, n, i * 3 + n, before)
                    split_lo(dve, p, j, i)
            p = PH_GLA_E
            for j in range(5):
                if j != 1:
                    n = (0, None, 1, 2, 0)[j]
                    saved = [PH_GLA_B.saved(1, 3), None, PH_GLA_B.saved(3, 3), PH_GLA_B.saved(5, 3), p.saved(1)][j]
                    gated(p, j, j, 0, n, 12 + (0, 0, 1, 2, 3)[j], saved)
                else:
                    dve.wait_ge(projected, p.c(j) + 1)
                split_lo(dve, p, j)

            SC = float(E) ** -0.5

            def dil_bias(h, g):
                dve.wait_ge(*P_DIL.at(f"s_{g}", h))
                if g == 0:
                    dve.wait_ge(bt_in, h * 16 + 16)
                late = (bank[3][:, 0:NP], bank[3][:, NP:2 * NP], bank[4][:, 0:NP])[g]
                nc.vector.scalar_tensor_tensor(out=s1[:, g, :], in0=late, scalar=SC, in1=btab[:, g, :],
                                               op0=ALU.mult, op1=ALU.add).then_inc(V_DIL(f"b1_{g}"), 1)
                nc.vector.scalar_tensor_tensor(out=s0[:, g, :], in0=bank[5][:, g * P:g * P + P], scalar=SC,
                                               in1=btab[:, g, P:NP], op0=ALU.mult, op1=ALU.add)\
                    .then_inc(V_DIL(f"b0_{g}"), 1)

            def dil_qk(h, g, st, saved):
                dve.wait_ge(*(P_DT if g == 2 else P_DIL).at(f"qs{g}", h))
                dve.wait_ge(*saved)
                nc.vector.tensor_copy(qkvs[:, g, :], bank[7][0:NS, 0:384]).then_inc(st(f"qk{g}"), 1)

            def dil_cached(h, g, st):
                n = DSLOTS[g]
                dve.wait_ge(qb_in, h * 48 + (16 * g + 16))
                dve.wait_ge(*((k2_in, h * 16 + 16) if g == 2 else (k_in, h * 32 + (16 * g + 16))))
                nc.vector.tensor_tensor(kcache[0:n, :, :], kcache[0:n, :, :], qspread[0:n, :, :], ALU.mult)\
                    .then_inc(st(f"m{g}"), 1)
                dve.wait_ge(*st.at(f"m{g}", h))
                nc.vector.tensor_reduce(sct[0:n, g, :], kcache[0:n, :, :], AX.X, ALU.add).then_inc(st(f"sc{g}"), 1)

            def dil_body(h, tail):
                p = PH_DIL
                for j in range(9):
                    split_lo(dve, p, j, h)
                    if j == 3:
                        dve.wait_ge(*V_DT.at("vn", h - 1))
                        dil_qk(h, 0, V_DIL, G_DIL.at("st0", h - 1))
                    tail(j)
                    if j % 3 == 2:
                        dil_bias(h, j // 3)
                    if j == 8:
                        dve.wait_ge(*V_DT.at("vn", h - 1))
                        dil_qk(h, 1, V_DIL, G_DIL.at("st1", h - 1))
                    if j == 5:
                        dil_cached(h, 0, V_DIL)
                    if j == 8:
                        dve.wait_ge(*V_DIL.at("b0_2", h))
                        for n, sc in enumerate((s1, s0)):
                            nc.vector.tensor_reduce(dst[:, n:n + 1], sc[:, :, :].rearrange("p g k -> p (g k)"), AX.X,
                                                    ALU.max, negate=True).then_inc(V_DIL(("mx1", "mx0")[n]), 1)
                        dve.wait_ge(*A_DIL.at("e0", h))
                        nc.vector.reciprocal(dst[:, 4:6], dst[:, 2:4]).then_inc(V_DIL("rc"), 1)
                        dve.wait_ge(*V_DIL.at("rc", h))
                        for n, sc in enumerate((s1, s0)):
                            nc.vector.tensor_scalar(sc[:, :, :], sc[:, :, :], dst[:, 4 + n:5 + n], None, ALU.mult)\
                                .then_inc(V_DIL(("n1", "n0")[n]), 1)

            def dil_tail(k, h):
                if k == 0:
                    dil_qk(h, 2, V_DT, G_DT.at("st2", h - 1))
                if k == 1:
                    dve.wait_ge(*P_DT.at("pt1", h))
                    nc.vector.tensor_copy(pT[:, 1, :], bank[4][:, 0:384]).then_inc(V_DT("pt1"), 1)
                    dil_cached(h, 1, V_DT)
                if k == 2:
                    dve.wait_ge(*A_DT.at("yh", h))
                    row = ds(h, 1)
                    nc.vector.tensor_tensor(y_lo[:, row, 0:NP], bank[7][:, None, 0:NP], y_hi[:, row, 0:NP].bitcast(F32),
                                            ALU.subtract).then_inc(V_DT("yl"), 1)
                    dve.wait_ge(*V_DT.at("qk2", h))
                    for g in range(3):
                        if g:
                            dve.wait_ge(*V_DT.at(f"nw{g - 1}", h))
                        nc.vector.tensor_tensor_reduce(out=qk_junk[:, :], in0=qkvs[:, g, 0:E], in1=qkvs[:, g, E:2 * E],
                                                       scale=1.0, scalar=0.0, op0=ALU.mult, op1=ALU.add,
                                                       accum_out=snew[:, g:g + 1]).then_inc(V_DT(f"nw{g}"), 1)
                    dve.wait_ge(*P_DT.at("pvs", h - 1))
                    nc.vector.tensor_copy(vnew[:, :, :], qkvs[:, :, 2 * E:3 * E]).then_inc(V_DT("vn"), 1)
                if k == 3:
                    dil_cached(h, 2, V_DT)
                if k == 5:
                    dve.wait_ge(*P_DT.at("sct", h))
                    dve.wait_ge(*V_DT.at("nw2", h))
                    dve.wait_ge(bs_in, h * 16 + 16)
                    dve.wait_ge(*P_DT.at("pst", h - 1))
                    nc.vector.scalar_tensor_tensor(out=ssamp[:, 0:SSEEN], in0=bank[7][0:NS, 0:SSEEN], scalar=SC,
                                                   in1=bsamp[:, 0:SSEEN], op0=ALU.mult, op1=ALU.add)\
                        .then_inc(V_DT("sb"), 1)
                    nc.vector.scalar_tensor_tensor(out=ssamp[:, SSEEN:SSEEN + 3], in0=snew[:, 0:3], scalar=SC,
                                                   in1=bsamp[:, SSEEN:SSEEN + 3], op0=ALU.mult, op1=ALU.add)\
                        .then_inc(V_DT("sbn"), 1)
                    dve.wait_ge(*V_DT.at("sbn", h))
                    nc.vector.tensor_reduce(dss[:, 0:1], ssamp[:, 0:SSEEN + 3], AX.X, ALU.max, negate=True)\
                        .then_inc(V_DT("smx"), 1)
                    dve.wait_ge(*A_DT.at("se", h))
                    nc.vector.reciprocal(dss[:, 2:3], dss[:, 1:2]).then_inc(V_DT("src"), 1)
                    dve.wait_ge(*V_DT.at("src", h))
                    nc.vector.tensor_scalar(ssamp[:, 0:SSEEN + 3], ssamp[:, 0:SSEEN + 3], dss[:, 2:3], None, ALU.mult)\
                        .then_inc(V_DT("sn"), 1)
                    dve.wait_ge(*V_DT.at("sn", h))
                    for g in range(3):
                        nc.vector.tensor_scalar(pdiag[:, g, :], ident[0:NS, 0:NS], ssamp[:, SSEEN + g:SSEEN + g + 1],
                                                None, ALU.mult).then_inc(V_DT(f"dg{g}"), 1)
                if k == 7:
                    dve.wait_ge(*A_DT.at("yhs", h))
                    row = ds(h, 1)
                    nc.vector.tensor_tensor(y_lo[:, row, NP:T], bank[7][:, None, 32:40],
                                            y_hi[:, row, NP:T].bitcast(F32), ALU.subtract).then_inc(V_DT("yls"), 1)

            dil_body(0, lambda k: None)
            with dve.Fori(1, 8) as h:
                dil_body(h, lambda k: dil_tail(k, h - 1))

            def pair_sums(p_g, p_b, p_e, ring, tmp, tail, B, E_, early=None):
                for j in range(4):
                    if j < 3:
                        split_lo(dve, p_g, j)
                    tail(j)
                    if j == 3:
                        split_lo(dve, p_g, j)
                for k in range(4, 8):
                    tail(k)

                def pair(p, j, k, i, g0, n, S, s0, gate_wait):
                    dve.wait_ge(projected, p.c(j, i) + 1)
                    for r in range(2):
                        dve.wait_ge(*gate_wait(g0 + r))
                        if S is E_ and s0 == 0:
                            dve.wait_ge(*B.at(f"add{r + 2}", 2))
                        else:
                            dve.wait_ge(*S.at(f"add{(s0 + r + 2) % 4}", i if s0 else i - 1))
                        nc.vector.tensor_tensor(tmp[:, r, :], ring[:, g0 + r, :], bank[p.outs[k + r]][:, 0:T], ALU.mult)\
                            .then_inc(evac[p.outs[k + r]], 1)
                        dve.wait_ge(*p.saved(k + r, i))
                        m = merged[:, ds(n + r, 1), :]
                        nc.vector.tensor_tensor(m, m, tmp[:, r:r + 1, :], ALU.add).then_inc(S(f"add{s0 + r}"), 1)
                with dve.Fori(0, 3) as i:
                    for j in range(6):
                        q = j // 3
                        if j % 3 == 0:
                            pair(p_b, j, 4 * q, i, 2 * q, i * 4 + 2 * q, B, 2 * q, lambda r: p_b.before(GATE_BANKS[r], i))
                        split_lo(dve, p_b, j, i)
                if early:
                    early()
                for q in range(2):
                    pair(p_e, q, 2 * q, 0, 2 * q, 12 + 2 * q, E_, 2 * q, lambda r: p_b.before(GATE_BANKS[r], 3))
                    if p_e.c(q) + RING < SLOTS:
                        split_lo(dve, p_e, q)
            pair_sums(PH_DIL_G, PH_DIL_B, PH_DIL_E, gates2, dtmp, lambda k: dil_tail(k, 7), V_DB, V_DE)

            def pool_finish(g):
                dve.wait_ge(*A_PO.at(f"d{g}"))
                nc.vector.tensor_tensor(y_lo[:, 8 + 2 * g:10 + 2 * g, :], pdiff[:, :, :],
                                        y_hi[:, 8 + 2 * g:10 + 2 * g, :].bitcast(F32), ALU.subtract)\
                    .then_inc(V_PO(f"l{g}"), 1)

            def pool_rows(g):
                dve.wait_ge(*P_PO.at(f"o{g}"))
                out = bank[4 + 2 * (g % 2)]
                nc.vector.tensor_copy(utok[:, g * 2 * P:(g + 1) * 2 * P], out[0:15, 0:NP]).then_inc(V_PO(f"ua{g}"), 1)
                nc.vector.tensor_copy(utok_s[:, g * 2 * P:(g + 1) * 2 * P], out[0:NS, NP:2 * NP])\
                    .then_inc(V_PO(f"ub{g}"), 1)

            nc.vector.tensor_tensor_scan(cinv[:, :], ones[:, 0:16], ones[:, 0:16], 0.0, ALU.mult, ALU.add)\
                .then_inc(V_PO("pos"), 1)
            dve.wait_ge(*V_PO.at("pos"))
            nc.vector.reciprocal(cinv[:, :], cinv[:, :]).then_inc(V_PO("cinv"), 1)
            for j in range(8):
                g = j // 2
                split_lo(dve, PH_PU, j)
                if j % 2 == 0:
                    if g:
                        pool_finish(g - 1)
                        pool_rows(g - 1)
                    continue
                w, u = 2 << g, u_ctx[:, 2 * (g % 2):2 * (g % 2) + 2, :]
                src = u
                dve.wait_ge(*A_PO.at(f"h{g}"))
                for k in range(g + 1):
                    if k:
                        dve.wait_ge(*V_PO.at(f"w{g}_{k - 1}"))
                    first, by = (2 << k) - 1, 1 << k
                    nc.vector.tensor_tensor(wsum[k % 2][:, :, first:UW], src[:, :, first:UW],
                                            src[:, :, first - by:UW - by], ALU.add).then_inc(V_PO(f"w{g}_{k}"), 1)
                    src = wsum[k % 2]
                dve.wait_ge(*V_PO.at(f"w{g}_{g}"))
                early = src[:, :, UP:UP + w - 1]
                nc.vector.scalar_tensor_tensor(out=early, in0=early, scalar=float(w),
                                               in1=cinv[:, None, 0:w - 1].to_broadcast([P, 2, w - 1]),
                                               op0=ALU.mult, op1=ALU.mult).then_inc(V_PO(f"f{g}"), 1)
                dve.wait_ge(*V_PO.at(f"f{g}"))
                for name, out, c in ((f"dp{g}", pdiff[:, :, 0:NP], slice(UP, UP + NP)),
                                     (f"ds{g}", pdiff[:, :, NP:T], slice(US + 15, US + 16 * NS, 16))):
                    nc.vector.scalar_tensor_tensor(out=out, in0=src[:, :, c], scalar=1.0 / w, in1=u[:, :, c],
                                                   op0=ALU.mult, op1=ALU.subtract).then_inc(V_PO(name), 1)
            pool_finish(3)

            def pool_scaled(k):
                if k != 4:
                    return
                for t in range(8):
                    b = PH_PW.outs[t]
                    dve.wait_ge(*A_PO.at(f"y{t}"))
                    nc.vector.scalar_tensor_tensor(out=y_lo[:, t, :], in0=bank[b][:, 0:T], scalar=param(PC_PSCALE, t),
                                                   in1=y_hi[:, t, :].bitcast(F32), op0=ALU.mult, op1=ALU.subtract)\
                        .then_inc(evac[b], 1)
                pool_rows(3)
                split_lo(dve, PH_PW, 0)

            def merged_lo(c):
                dve.wait_ge(*A_MH.at(f"m{c}"))
                nc.vector.tensor_tensor(h_lo[:, 4 * c:4 * c + 4, :], merged[:, 4 * c:4 * c + 4, :],
                                        h_hi[:, 4 * c:4 * c + 4, :].bitcast(F32), ALU.subtract).then_inc(V_MH(f"m{c}"), 1)

            def merged_early():
                for c in range(3):
                    merged_lo(c)
            pair_sums(PH_PL_G, PH_PL_B, PH_PL_E, gates2, dtmp, pool_scaled, V_PB, V_PE, merged_early)
            merged_lo(3)
            nc.vector.memset(acc[:, :], 0.0).then_inc(V_MH("zero"), 1)
            dve.wait_ge(*V_MH.at("zero"))

            def add_squares(p, S, j, k, i, before):
                dve.wait_ge(*p.saved(k, i))
                dve.wait_ge(*before)
                nc.vector.tensor_tensor(acc[:, :], acc[:, :], sqr[:, k % 3, :], ALU.add).then_inc(V_OUT[S](f"acc{k}"), 1)

            def mix_body(i):
                for j in range(3):
                    add_squares(PH_MO, "mix", j, j, i, V_OUT["mix"].at(f"acc{(j + 2) % 3}", i if j else i - 1))
                    split_lo(dve, PH_MO, j, i)
                    if isinstance(i, int) and j == 2:
                        dve.wait_ge(*A_MM.at("s1"))
                        nc.vector.tensor_scalar(mstat[:, 2:4], mstat[:, 0:2], 1.0 / D, EPS, ALU.mult, ALU.add)\
                            .then_inc(V_MM("var"), 1)
                        dve.wait_ge(*A_MM.at("root"))
                        nc.vector.reciprocal(mstat[:, 6:8], mstat[:, 4:6]).then_inc(V_MM("rstd"), 1)
            mix_body(0)
            with dve.Fori(1, 3) as i:
                mix_body(i)
            for t in range(KB):
                dve.wait_ge(*A_MM.at(f"hi{t}"))
                nc.vector.scalar_tensor_tensor(out=hm_lo[:, t, :], in0=bank[3 + t % 4][:, 0:NP], scalar=param(PC_MEM, t),
                                               in1=hm_hi[:, t, :].bitcast(F32), op0=ALU.mult, op1=ALU.subtract)\
                    .then_inc(V_MM(f"lo{t}"), 1)
            with dve.Fori(3, 5) as i:
                mix_body(i)
            add_squares(PH_MO_E, "mix_end", 0, 0, 0, V_OUT["mix"].at("acc2", 4))
            split_lo(dve, PH_MO_E, 0)

            def y_rows(c):
                dve.wait_ge(*P_Y.at(f"y{c}"))
                nc.vector.tensor_copy(ytok[:, 1, c * 512:c * 512 + 512], bank[(4, 7)[c % 2]][:, :]).then_inc(V_Y(f"y{c}"), 1)

            def norm(n, g_post, g_pre):
                V, A_, Pn = V_N[n], A_N[n], P_N[n]

                def root(tag, name, wait):
                    dve.wait_ge(*wait)
                    nc.vector.tensor_scalar(rstd[:, :], bank[7][:, 0:T], 1.0 / D, EPS, ALU.mult, ALU.add)\
                        .then_inc(V(f"var{tag}"), 1)
                    dve.wait_ge(*A_.at(f"root{tag}"))
                    nc.vector.reciprocal(rstd[:, :], rstd[:, :]).then_inc(V(f"rstd{tag}"), 1)
                    dve.wait_ge(*V.at(f"rstd{tag}"))
                spread = rstd[:, None, :].to_broadcast([P, 4, T])
                root("", "var", Pn.at("sum"))
                for c in range(4):
                    m = merged[:, 4 * c:4 * c + 4, :]
                    nc.vector.tensor_tensor(m, m, spread, ALU.mult).then_inc(V(f"yr{c}"), 1)
                    dve.wait_ge(*V.at(f"yr{c}"))
                    for t in range(4 * c, 4 * c + 4):
                        if n == 0:
                            dve.wait_ge(*Pn.at(f"xt{t}"))
                        old = bank[3 + t % 3][:, 0:T] if n == 0 else xres[:, t, :]
                        nc.vector.scalar_tensor_tensor(out=xres[:, t, :], in0=merged[:, t, :], scalar=param(g_post, t),
                                                       in1=old, op0=ALU.mult, op1=ALU.add).then_inc(V(f"x{t}"), 1)
                    if n == 2 and c:
                        y_rows(c - 1)
                if n == 2:
                    return
                root("2", "var2", Pn.at("s15"))

                def low(c):
                    for t in range(4 * c, 4 * c + 4):
                        dve.wait_ge(*A_.at(f"hi{t}"))
                        nc.vector.scalar_tensor_tensor(out=h_lo[:, t, :], in0=merged[:, t, :], scalar=param(g_pre, t),
                                                       in1=h_hi[:, t, :].bitcast(F32), op0=ALU.mult, op1=ALU.subtract)\
                            .then_inc(V(f"lo{t}"), 1)

                def scaled(c):
                    nc.vector.tensor_tensor(merged[:, 4 * c:4 * c + 4, :], xres[:, 4 * c:4 * c + 4, :], spread, ALU.mult)\
                        .then_inc(V(f"t{c}"), 1)

                def zero():
                    nc.vector.memset(acc[:, :], 0.0).then_inc(V("zero"), 1)
                if n == 0:
                    return scaled, low, zero
                for c in range(4):
                    scaled(c)
                    if c:
                        low(c - 1)
                low(3)
                zero()
            scaled, low, zero = norm(0, PC_MIXPOST, PC_XPRE)

            def kv_tile(p, j, i, key=None):
                split_lo(dve, p, j, i)
                if key:
                    dve.wait_ge(*p.saved(j, i))
                    nc.vector.tensor_copy(key[0][:, key[1]:key[1] + 1, :], kvr[:, j:j + 1, :]).then_inc(V_KK(f"k{j}"), 1)

            def kv_turned(Pt, V, j, i, kv, n):
                dve.wait_ge(*Pt.at(f"t{j}", i))
                nc.vector.tensor_copy(kvtok2[:, kv, :, ds(n * P, P)],
                                      bank[6][:, 0:NP].rearrange("p (m e) -> p m e", e=P)).then_inc(V(f"t{j}"), 1)
            for i in range(3):
                for j in range(3):
                    n = 3 * i + j
                    kv_tile(PH_KV, j, i, (kT[n // 4], n % 4) if n < 8 else None)
                    if n < 4:
                        scaled(n)
                    if n:
                        kv_turned(P_KV, V_KV, (j + 2) % 3, (n - 1) // 3, 0, n - 1)
                    if n < 4:
                        low(n)
                    if n == 4:
                        zero()
            with dve.Fori(3, 5) as i:
                for j in range(3):
                    kv_tile(PH_KV, j, i)
                    kv_turned(P_KV, V_KV, (j + 2) % 3, i if j else i - 1, 1, i * 3 + (j - 9))
            kv_tile(PH_KV_E, 0, 0)
            kv_turned(P_KV, V_KV, 2, 4, 1, 6)
            kv_turned(P_KE, V_KE, 0, 0, 1, 7)

            def cached(h, b, mt):
                dve.wait_ge(kc_in[b // 4], (h + 1) * NS // 2 * 16)
                return nc.vector.tensor_tensor_reduce(
                    out=kc2[:, b, mt, :], in0=kc2[:, b, mt, :], in1=bank[5 + (b // 2) % 2][:, (b % 2) * NP:(b % 2 + 1) * NP],
                    scale=1.0, scalar=0.0, op0=ALU.mult, op1=ALU.add, accum_out=xsct[:, mt, b:b + 1])

            def x_piece(p, h):
                if p == 0:
                    dve.wait_ge(*P_X.at(f"sc_{h}"))
                    nc.vector.tensor_reduce(xst[:, 0:2], bank[3][:, :].rearrange("p (m k) -> p m k", k=NP), AX.X, ALU.max,
                                            negate=True).then_inc(V_X(f"mx_{h}"), 1)
                    dve.wait_ge(*V_X.at(f"mx_{h}"))
                    nc.vector.tensor_scalar(xst[:, 2:4], xst[:, 0:2], 1.0 / 16, None, ALU.mult).then_inc(V_X(f"mxs_{h}"), 1)
                    dve.wait_ge(*A_X.at(f"e1_{h}"))
                    nc.vector.reciprocal(xst[:, 6:8], xst[:, 4:6]).then_inc(V_X(f"rc_{h}"), 1)
                    dve.wait_ge(*V_X.at(f"rc_{h}"))
                    for m in range(2):
                        nc.vector.tensor_scalar(xp[:, m, :], xp[:, m, :], xst[:, 6 + m:7 + m], None, ALU.mult)\
                            .then_inc(V_X(f"n{m}_{h}"), 1)
                if p in (1, 2):
                    if p == 2:
                        dve.wait_ge(*A_X.at(f"oh_{h}"))
                        nc.vector.tensor_tensor(o_lo[:, 2 * h:2 * h + 2, 0:NP],
                                                bank[4][:, :].rearrange("p (t q) -> p t q", q=NP),
                                                o_hi[:, 2 * h:2 * h + 2, 0:NP].bitcast(F32), ALU.subtract)\
                            .then_inc(V_X(f"ol_{h}"), 1)
                    for n in (2 * p - 2, 2 * p - 1):
                        dve.wait_ge(*P_X.at(f"sp{n}_{h}"))
                        for k in range(2):
                            for mt in range(2):
                                b = 2 * n + k
                                if h and mt == 0 and b == 0:
                                    dve.wait_ge(*P_X.at(f"sct_{h - 1}"))
                                ins = cached(h, b, mt)
                            ins.then_inc(V_X(f"k{b}_{h}"), 1)
                if p == 3:
                    dve.wait_ge(*P_X.at(f"sct_{h}"))
                    nc.vector.tensor_reduce(xss[:, 0:1], bank[7][0:NS, 0:NP], AX.X, ALU.max, negate=True)\
                        .then_inc(V_X(f"smx_{h}"), 1)
                    dve.wait_ge(*V_X.at(f"smx_{h}"))
                    nc.vector.tensor_scalar(xss[:, 1:2], xss[:, 0:1], 1.0 / 16, None, ALU.mult).then_inc(V_X(f"smxs_{h}"), 1)
                    dve.wait_ge(*A_X.at(f"se_{h}"))
                    nc.vector.reciprocal(xss[:, 3:4], xss[:, 2:3]).then_inc(V_X(f"src_{h}"), 1)
                    dve.wait_ge(*V_X.at(f"src_{h}"))
                    nc.vector.tensor_scalar(ssx[:, :], ssx[:, :], xss[:, 3:4], None, ALU.mult).then_inc(V_X(f"sn_{h}"), 1)
                if p == 5:
                    dve.wait_ge(*A_X.at(f"ohs_{h}"))
                    nc.vector.tensor_tensor(o_lo[:, 2 * h:2 * h + 2, NP:T],
                                            bank[7][:, 272:288].rearrange("p (t b) -> p t b", b=NS),
                                            o_hi[:, 2 * h:2 * h + 2, NP:T].bitcast(F32), ALU.subtract)\
                        .then_inc(V_X(f"ols_{h}"), 1)
            for s, pieces in enumerate(X_ORDER):
                if s < 8:
                    split_lo(dve, PH_XQ, s)
                for p, h in pieces:
                    x_piece(p, h)

            def xo_slot(p, S, j, i):
                for r in range(2):
                    k = 2 * j + r
                    if S == "xo":
                        before = V_OUT["xo"].at(f"acc{(k + 5) % 6}", i if k else i - 1)
                    else:
                        before = V_OUT[S].at(f"acc{k - 1}") if k else V_OUT["xo"].at("acc5", 1)
                    add_squares(p, S, j, k, i, before)
                split_lo(dve, p, j, i)
            with dve.Fori(0, 2) as i:
                for j in range(3):
                    xo_slot(PH_XO, "xo", j, i)
            for j in range(2):
                xo_slot(PH_XO_E, "xo_end", j, 0)
            norm(1, PC_XPOST, PC_FPRE)
            for c in range(4):
                dve.wait_ge(*P_H.at(f"h{c}"))
                nc.vector.tensor_copy(hist[:, 4 * c:4 * c + 4, :],
                                      bank[3 + c][:, 0:8 * FT].rearrange("p (r t) -> p r t", r=4)).then_inc(V_H(f"h{c}"), 1)
            dve.wait_ge(*V_H.at("h3"))

            for half, (up, up_e, down, down_e) in enumerate(PH_FFN):
                def conv(p, S, V, j, i, n):
                    kind, q = j % 2, j // 2
                    col = half * FH + kind * FT
                    c, u = (cg, cv)[kind][:, q, :], bank[p.outs[j]]
                    dve.wait_ge(*S.at(f"n{j}", i))
                    old = hist[:, :, ds(n + col, 1)].rearrange("p (b r) a -> p r (b a)", r=2)

                    def tap(k, out, src):
                        return nc.vector.scalar_tensor_tensor(out=out, in0=src, scalar=param(PC_CW + 88 * k + col, n),
                                                              in1=out, op0=ALU.mult, op1=ALU.add)
                    tap(1, c[:, NP:T], old[:, 1, :]).then_inc(V(f"s{j}"), 1)
                    tap(1, c[:, 1:NP], u[:, 0:NP - 1]).then_inc(V(f"r{j}"), 1)
                    dve.wait_ge(*V.at(f"r{j}", i))
                    tap(0, c[:, NP:T], old[:, 0, :]).then_inc(V(f"w{j}"), 1)
                    tap(0, c[:, 2:NP], u[:, 0:NP - 2]).then_inc(evac[p.outs[j]], 1)
                    if kind:
                        dve.wait_ge(*S.at(f"g{q}", i))
                        dve.wait_ge(*p.saved(j, i))
                        v = cv[:, q:q + 1, :]
                        nc.vector.tensor_tensor(v, cg[:, q:q + 1, :], v, ALU.mult).then_inc(V(f"m{q}"), 1)
                        dve.wait_ge(*S.at(f"hi{q}", i))
                        nc.vector.tensor_tensor(y_lo[:, ds(n, 1), :], v, y_hi[:, ds(n, 1), :].bitcast(F32), ALU.subtract)\
                            .then_inc(V(f"lo{q}"), 1)
                    split_lo(dve, p, j, i)
                with dve.Fori(0, 7) as i:
                    for j in range(6):
                        conv(up, A_F[half], V_F[half], j, i, i * 3 + j // 2)
                for j in range(2):
                    conv(up_e, A_FE[half], V_FE[half], j, 0, 21)

                def down_tile(p, S, k, i, n):
                    for r in range(2):
                        if more(p, 2 * k + r, i):
                            split_lo(dve, p, 2 * k + r, i)
                        elif r:
                            dve.wait_ge(projected, p.c(2 * k + r, i) + 1)
                        if r and half == 1:
                            m = merged[:, ds(n, 1), :]
                            nc.vector.tensor_tensor(m, m, bank[p.outs[k]][:, None, 0:T], ALU.add)\
                                .then_inc(evac[p.outs[k]], 1)
                            dve.wait_ge(*A_OUT[S].at(f"sq{k}", i))
                            if S == "down":
                                dve.wait_ge(*V_OUT[S].at(f"acc{(k + 2) % 3}", i if k else i - 1))
                            else:
                                dve.wait_ge(*V_OUT["down"].at("acc2", 4))
                            nc.vector.tensor_tensor(acc[:, :], acc[:, :], sqr[:, k, :], ALU.add)\
                                .then_inc(V_OUT[S](f"acc{k}"), 1)
                with dve.Fori(0, 4) as i:
                    for k in range(3):
                        down_tile(down, "down", k, i, i * 3 + k)
                for k in range(3):
                    down_tile(down, "down", k, 4, 12 + k)
                if half == 1:
                    for c in range(5):
                        dve.wait_ge(*P_Y.at(f"c{c}"))
                        nc.vector.tensor_copy(newtok[:, 2 * c:2 * c + 2, :],
                                              bank[3 + c][0:2 * FT, 0:NP].rearrange("p (r e) -> p r e", e=P))\
                            .then_inc(V_Y(f"c{c}"), 1)
                down_tile(down_e, "down_end", 0, 0, 15)
            norm(2, PC_FPOST, None)
            y_rows(3)


_INS = ["x_prompt", "x_sample", "state_pool", "cache_dil1_kv", "cache_dil2_kv", "cache_dil3_kv", "state_gla",
        "cache_mem_kv", "state_ffn_conv", "mem_prompt", "rel_bias", "norm_mix_pre", "norm_mix_post", "w_in", "pool_w",
        "pool_scale", "gla_w_a2", "gla_b_a", "gla_norm", "w_br_pool", "w_br_dil", "w_br_gla", "w_mix_out",
        "norm_x_pre", "norm_x_post", "norm_mem", "w_xq", "w_xkv", "w_xo", "norm_ffn_pre", "norm_ffn_post", "w_up",
        "conv_w", "conv_b", "w_down"]
_OUTS = [("y_p", (1, NP, D)), ("y_s", (NS, 1, D)), ("pool_p", (1, 1, 15, 1024)),
         ("dil1_p", (1, 1, 128, 2, H, E)), ("dil2_p", (1, 1, NP, 2, H, E)), ("dil3_p", (1, 1, NP, 2, H, E)),
         ("gla_p", (1, 1, 4, 256, 512)), ("mem_p", (1, 1, 256, 2, 4, 256)), ("conv_p", (1, 1, 2, 2 * DF)),
         ("pool_s", (1, NS, 15, 1024)), ("dil1_s", (1, NS, 1, 2, H, E)), ("dil2_s", (1, NS, 1, 2, H, E)),
         ("dil3_s", (1, NS, 1, 2, H, E)), ("gla_s", (1, NS, 4, 256, 512)), ("conv_s", (1, NS, 2, 2 * DF))]


def bias_onehot():
    def bucket(dist):
        scaled = np.log(np.float32(max(dist, 1)) / np.float32(16)) / np.float32(np.log(2048 / 16))
        return dist if dist < 16 else min(16 + int(scaled * 16), 31)
    out = np.zeros((33, 3 * 383 + SSEEN + 3), np.float32)
    for g, dil in enumerate(DILS):
        for m in range(383):
            d = 255 - m
            seen = d >= 0 and d % dil == 0 and d // dil <= 128
            out[bucket(d) if seen else 32, 383 * g + m] = 1
    col = 3 * 383
    for g, dil in enumerate(DILS):
        for r in range(DSLOTS[g]):
            out[bucket((DSLOTS[g] - r) * dil), col] = 1
            col += 1
    out[0, col:col + 3] = 1
    return out


def kernel(**inputs):
    import concourse.bacc as _bacc
    from concourse.bass_utils import run_bass_kernel_spmd as _run

    nc = _bacc.Bacc("TRN2", target_bir_lowering=False, num_devices=1)
    arrays, A = {}, {}
    for name in _INS + ["onehot"]:
        a = np.ascontiguousarray(inputs[name]) if name != "onehot" else bias_onehot()
        arrays[f"in_{name}"] = a
        A[name] = nc.dram_tensor(f"in_{name}", a.shape, mybir.dt.from_np(a.dtype), kind="ExternalInput").ap()
    for name, shape in _OUTS:
        A[name] = nc.dram_tensor(f"out_{name}", shape, F32, kind="ExternalOutput").ap()
    build(nc, A)
    r = _run(nc, [arrays], core_ids=[0])
    return tuple(r.results[0][f"out_{name}"] for name, _ in _OUTS)
```
